# Optimizing a Trainium2 kernel written in Bass

```python
import math
import jax, jax.numpy as jnp
from jax import lax
import numpy as np

D_MODEL = 1024
BATCH = 1
SEQ = 256
DEPTH = 1

SSD_HEADS = 16
SSD_HEAD_DIM = 64
SSD_INNER = SSD_HEADS * SSD_HEAD_DIM
SSD_GROUPS = 2
SSD_STATE = 128
SSD_CONV = 4
SSD_CHUNK = 128
CONV_CH = SSD_INNER + 2 * SSD_GROUPS * SSD_STATE
SB_HEADS = 8
SB_HEAD_DIM = 64
SB_INNER = SB_HEADS * SB_HEAD_DIM
SB_BLOCK = 128
N_BRANCH = 2
MEM_LEN = 256
XA_HEADS = 4
XA_HEAD_DIM = 128
XA_INNER = XA_HEADS * XA_HEAD_DIM
N_EXPERTS = 32
TOP_K = 4
D_FF = D_MODEL
SWIGLU_LIMIT = 7.0
SWIGLU_ALPHA = 1.702
MOE_BLOCK = 256
EPS = 1e-6
SPLIT_Z = SSD_INNER
SPLIT_XBC = SPLIT_Z + CONV_CH
SPLIT_DT = SPLIT_XBC + SSD_HEADS
SPLIT_Q = SPLIT_DT + SB_INNER
SPLIT_K = SPLIT_Q + SB_INNER
SPLIT_V = SPLIT_K + SB_INNER
N_IN = SPLIT_V + N_BRANCH * D_MODEL

kernel_name = "hybrid_ssd_stickbreak_moe_block"

def rms_norm(x, g):
    xf = x.astype(jnp.float32)
    y = xf * lax.rsqrt(jnp.mean(xf * xf, axis=-1, keepdims=True) + EPS)
    return (y * g.astype(jnp.float32)).astype(x.dtype)

def causal_dwconv(u, w, b):
    c = u.shape[-1]
    y = lax.conv_general_dilated(u, w[:, None, :].astype(u.dtype), window_strides=(1,),
                                 padding=[(SSD_CONV - 1, 0)],
                                 dimension_numbers=('NWC', 'WIO', 'NWC'),
                                 feature_group_count=c)
    return y + b

def segsum(a):
    t = a.shape[-1]
    cs = jnp.cumsum(a, axis=-1)
    diff = cs[..., :, None] - cs[..., None, :]
    mask = jnp.tril(jnp.ones((t, t), dtype=bool))
    return jnp.where(mask, diff, -jnp.inf)

def ssd_chunked(xh, dt, a, bm, cm):
    bsz, s, h, p = xh.shape
    g, n = bm.shape[-2:]
    r = h // g
    c = s // SSD_CHUNK
    l = SSD_CHUNK
    dtype = xh.dtype
    xdt = (xh * dt[..., None].astype(dtype)).reshape(bsz, c, l, g, r, p)
    da = (dt * a).reshape(bsz, c, l, g, r).transpose(0, 3, 4, 1, 2)
    da_cs = jnp.cumsum(da, axis=-1)
    bc = bm.reshape(bsz, c, l, g, n)
    cc = cm.reshape(bsz, c, l, g, n)
    lmat = jnp.exp(segsum(da)).astype(dtype)
    cb = jnp.einsum('bclgn,bcsgn->bgcls', cc, bc)
    y_diag = jnp.einsum('bgrcls,bcsgrp->bclgrp', cb[:, :, None] * lmat, xdt)
    decay_states = jnp.exp(da_cs[..., -1:] - da_cs).astype(dtype)
    xw = xdt * decay_states.transpose(0, 3, 4, 1, 2)[..., None]
    states = jnp.einsum('bclgn,bclgrp->bcgrpn', bc, xw)
    chunk_tot = jnp.pad(da_cs[..., -1], ((0, 0), (0, 0), (0, 0), (1, 0)))
    decay_chunk = jnp.exp(segsum(chunk_tot)).astype(dtype)
    states0 = jnp.concatenate([jnp.zeros_like(states[:, :1]), states], axis=1)
    new_states = jnp.einsum('bgrzc,bcgrpn->bzgrpn', decay_chunk, states0)
    states_in = new_states[:, :-1]
    out_decay = jnp.exp(da_cs).astype(dtype).transpose(0, 3, 4, 1, 2)[..., None]
    y_off = jnp.einsum('bclgn,bcgrpn->bclgrp', cc, states_in) * out_decay
    return (y_diag + y_off).reshape(bsz, s, h, p)

def ssd_mixer(z, xbc_raw, dt_raw, conv_w, conv_b, dt_bias, a_log, d_skip, g_norm):
    bsz, s, _ = z.shape
    xbc = jax.nn.silu(causal_dwconv(xbc_raw, conv_w, conv_b))
    xs = xbc[..., :SSD_INNER]
    bm = xbc[..., SSD_INNER:SSD_INNER + SSD_GROUPS * SSD_STATE].reshape(bsz, s, SSD_GROUPS, SSD_STATE)
    cm = xbc[..., SSD_INNER + SSD_GROUPS * SSD_STATE:].reshape(bsz, s, SSD_GROUPS, SSD_STATE)
    xh = xs.reshape(bsz, s, SSD_HEADS, SSD_HEAD_DIM)
    dt = jax.nn.softplus(dt_raw.astype(jnp.float32) + dt_bias.astype(jnp.float32))
    a = -jnp.exp(a_log.astype(jnp.float32))
    y = ssd_chunked(xh, dt, a, bm, cm) + xh * d_skip[:, None]
    y = y.reshape(bsz, s, SSD_INNER) * jax.nn.silu(z)
    yg = rms_norm(y.reshape(bsz, s, SSD_GROUPS, SSD_INNER // SSD_GROUPS),
                  g_norm.reshape(SSD_GROUPS, SSD_INNER // SSD_GROUPS))
    return yg.reshape(bsz, s, SSD_INNER)

def stick_breaking_attention(q, k, v):
    bsz, s, h, dh = q.shape
    nb = s // SB_BLOCK
    scale = dh ** -0.5
    kt = k.transpose(0, 2, 1, 3)
    vt = v.transpose(0, 2, 1, 3)
    qb = q.reshape(bsz, nb, SB_BLOCK, h, dh).transpose(1, 0, 3, 2, 4)
    key_pos = jnp.arange(s)

    def block(args):
        q_blk, i = args
        q_pos = i * SB_BLOCK + jnp.arange(SB_BLOCK)
        logits = jnp.einsum('bhtd,bhsd->bhts', q_blk, kt).astype(jnp.float32) * scale
        mask = key_pos[None, :] < q_pos[:, None]
        log_beta = jax.nn.log_sigmoid(logits)
        log_stay = jnp.where(mask, jax.nn.log_sigmoid(-logits), 0.0)
        rev = lax.cumsum(log_stay, axis=3, reverse=True)
        after = jnp.concatenate([rev[..., 1:], jnp.zeros_like(rev[..., :1])], axis=-1)
        w = jnp.where(mask, jnp.exp(log_beta + after), 0.0)
        return jnp.einsum('bhts,bhsd->bthd', w.astype(vt.dtype), vt)

    out = lax.map(block, (qb, jnp.arange(nb)))
    return out.transpose(1, 0, 2, 3, 4).reshape(bsz, s, h * dh)

def memory_cross_attention(hn, memn, w_xq, w_xkv, w_xo):
    bsz, s, _ = hn.shape
    m = memn.shape[1]
    q = (hn @ w_xq).reshape(bsz, s, XA_HEADS, XA_HEAD_DIM)
    kv = memn @ w_xkv
    k = kv[..., :XA_INNER].reshape(bsz, m, XA_HEADS, XA_HEAD_DIM)
    v = kv[..., XA_INNER:].reshape(bsz, m, XA_HEADS, XA_HEAD_DIM)
    logits = jnp.einsum('bthd,bmhd->bhtm', q, k).astype(jnp.float32) * (XA_HEAD_DIM ** -0.5)
    p = jax.nn.softmax(logits, axis=-1).astype(v.dtype)
    o = jnp.einsum('bhtm,bmhd->bthd', p, v).reshape(bsz, s, XA_INNER)
    return o @ w_xo

def moe_ffn(hn, w_router, b_router, w_gu, b_gu, w_down, b_down):
    bsz, s, d = hn.shape
    t = bsz * s
    n_assign = t * TOP_K
    hf = hn.reshape(t, d)
    logits = (hf @ w_router + b_router).astype(jnp.float32)
    top_v, top_i = lax.top_k(logits, TOP_K)
    gate = jax.nn.softmax(top_v, axis=-1)
    e_flat = top_i.reshape(-1)
    tok_flat = jnp.arange(n_assign, dtype=jnp.int32) // TOP_K
    g_flat = gate.reshape(-1)
    order = jnp.argsort(e_flat)
    e_sorted = e_flat[order]
    tok_sorted = tok_flat[order]
    g_sorted = g_flat[order]
    counts = jnp.bincount(e_flat, length=N_EXPERTS)
    padded = (counts + MOE_BLOCK - 1) // MOE_BLOCK * MOE_BLOCK
    start = jnp.cumsum(counts) - counts
    pend = jnp.cumsum(padded)
    pstart = pend - padded
    rank = jnp.arange(n_assign, dtype=jnp.int32) - start[e_sorted]
    dest = pstart[e_sorted] + rank
    n_blocks = -(-n_assign // MOE_BLOCK) + N_EXPERTS
    n_rows = n_blocks * MOE_BLOCK
    row_tok = jnp.full((n_rows,), t, dtype=jnp.int32).at[dest].set(tok_sorted)
    row_gate = jnp.zeros((n_rows,), jnp.float32).at[dest].set(g_sorted)
    blk_start = jnp.arange(n_blocks) * MOE_BLOCK
    blk_expert = jnp.minimum(jnp.searchsorted(pend, blk_start, side='right'), N_EXPERTS - 1)
    xin = jnp.take(hf, row_tok, axis=0, mode='fill', fill_value=0).reshape(n_blocks, MOE_BLOCK, d)

    def expert_block(args):
        xb, e = args
        gu = xb @ w_gu[e] + b_gu[e]
        g_lin = jnp.minimum(gu[..., :D_FF], SWIGLU_LIMIT)
        u_lin = jnp.clip(gu[..., D_FF:], -SWIGLU_LIMIT, SWIGLU_LIMIT)
        act = g_lin * jax.nn.sigmoid(SWIGLU_ALPHA * g_lin) * (u_lin + 1.0)
        return act @ w_down[e] + b_down[e]

    yb = lax.map(expert_block, (xin, blk_expert)).reshape(n_rows, d)
    y = jnp.zeros((t, d), hn.dtype).at[row_tok].add(yb * row_gate[:, None].astype(yb.dtype), mode='drop')
    return y.reshape(bsz, s, d)

def setup_inputs(seed: int = 0) -> dict:
    key = jax.random.key(seed)
    ks = jax.random.split(key, 32)
    f32 = jnp.float32
    nrm = lambda k, shp, sc: jax.random.normal(k, shp, f32) * sc
    gain = lambda k, shp: 1.0 + 0.02 * jax.random.normal(k, shp, f32)
    u = jax.random.uniform(ks[5], (DEPTH, SSD_HEADS), f32)
    dt0 = jnp.exp(u * (math.log(0.1) - math.log(0.001)) + math.log(0.001))
    return {
        "x": nrm(ks[0], (BATCH, SEQ, D_MODEL), 1.0),
        "mem": nrm(ks[1], (BATCH, MEM_LEN, D_MODEL), 1.0),
        "g_mix": gain(ks[2], (DEPTH, D_MODEL)),
        "w_in": nrm(ks[3], (DEPTH, D_MODEL, N_IN), D_MODEL ** -0.5),
        "conv_w": nrm(ks[4], (DEPTH, SSD_CONV, CONV_CH), SSD_CONV ** -0.5),
        "conv_b": nrm(ks[6], (DEPTH, CONV_CH), 0.01),
        "dt_bias": dt0 + jnp.log(-jnp.expm1(-dt0)),
        "a_log": jnp.log(jax.random.uniform(ks[7], (DEPTH, SSD_HEADS), f32, 1.0, 16.0)),
        "d_skip": 1.0 + 0.1 * jax.random.normal(ks[8], (DEPTH, SSD_HEADS), f32),
        "g_ssd": gain(ks[9], (DEPTH, SSD_INNER)),
        "w_ssd_out": nrm(ks[10], (DEPTH, SSD_INNER, D_MODEL), SSD_INNER ** -0.5),
        "w_sb_out": nrm(ks[11], (DEPTH, SB_INNER, D_MODEL), SB_INNER ** -0.5),
        "w_out": nrm(ks[12], (DEPTH, D_MODEL, D_MODEL), D_MODEL ** -0.5),
        "g_xattn": gain(ks[13], (DEPTH, D_MODEL)),
        "g_mem": gain(ks[14], (DEPTH, D_MODEL)),
        "w_xq": nrm(ks[15], (DEPTH, D_MODEL, XA_INNER), D_MODEL ** -0.5),
        "w_xkv": nrm(ks[16], (DEPTH, D_MODEL, 2 * XA_INNER), D_MODEL ** -0.5),
        "w_xo": nrm(ks[17], (DEPTH, XA_INNER, D_MODEL), XA_INNER ** -0.5),
        "g_moe": gain(ks[18], (DEPTH, D_MODEL)),
        "w_router": nrm(ks[19], (DEPTH, D_MODEL, N_EXPERTS), D_MODEL ** -0.5),
        "b_router": nrm(ks[20], (DEPTH, N_EXPERTS), 0.01),
        "w_gu": nrm(ks[21], (DEPTH, N_EXPERTS, D_MODEL, 2 * D_FF), D_MODEL ** -0.5),
        "b_gu": nrm(ks[22], (DEPTH, N_EXPERTS, 2 * D_FF), 0.01),
        "w_down": nrm(ks[23], (DEPTH, N_EXPERTS, D_FF, D_MODEL), D_FF ** -0.5),
        "b_down": nrm(ks[24], (DEPTH, N_EXPERTS, D_MODEL), 0.01),
        "g_final": gain(ks[25], (D_MODEL,)),
    }

def reference(x, mem, g_mix, w_in, conv_w, conv_b, dt_bias, a_log, d_skip, g_ssd, w_ssd_out,
              w_sb_out, w_out, g_xattn, g_mem, w_xq, w_xkv, w_xo, g_moe, w_router, b_router,
              w_gu, b_gu, w_down, b_down, g_final):
    bsz, s, _ = x.shape
    h = x
    for i in range(DEPTH):
        n = rms_norm(h, g_mix[i])
        proj = n @ w_in[i]
        z = proj[..., :SPLIT_Z]
        xbc = proj[..., SPLIT_Z:SPLIT_XBC]
        dt_raw = proj[..., SPLIT_XBC:SPLIT_DT]
        q = proj[..., SPLIT_DT:SPLIT_Q].reshape(bsz, s, SB_HEADS, SB_HEAD_DIM)
        k = proj[..., SPLIT_Q:SPLIT_K].reshape(bsz, s, SB_HEADS, SB_HEAD_DIM)
        v = proj[..., SPLIT_K:SPLIT_V].reshape(bsz, s, SB_HEADS, SB_HEAD_DIM)
        gates = jax.nn.sigmoid(proj[..., SPLIT_V:])
        y_ssd = ssd_mixer(z, xbc, dt_raw, conv_w[i], conv_b[i], dt_bias[i], a_log[i],
                          d_skip[i], g_ssd[i]) @ w_ssd_out[i]
        y_sb = stick_breaking_attention(q, k, v) @ w_sb_out[i]
        merged = gates[..., :D_MODEL] * y_ssd + gates[..., D_MODEL:] * y_sb
        h = h + merged @ w_out[i]
        h = h + memory_cross_attention(rms_norm(h, g_xattn[i]), rms_norm(mem, g_mem[i]),
                                       w_xq[i], w_xkv[i], w_xo[i])
        h = h + moe_ffn(rms_norm(h, g_moe[i]), w_router[i], b_router[i], w_gu[i], b_gu[i],
                        w_down[i], b_down[i])
    return rms_norm(h, g_final)


_drawn_inputs = setup_inputs


def setup_inputs(seed=0):
    import zlib

    import numpy as np

    out = dict(_drawn_inputs(seed))
    spreads = {}
    factors = {'g_xattn': 6.092,
     'g_mem': 4.963,
     'b_gu': 44.394,
     'b_down': 51.048,
     'g_final': 7.864,
     'g_moe': 5.246,
     'b_router': 6.565}
    for name, (base, spread) in spreads.items():
        noise = np.random.default_rng([zlib.crc32(name.encode()), seed]).standard_normal(out[name].shape)
        drawn = base * np.exp(spread * noise) if base else spread * noise
        out[name] = __import__('jax').numpy.asarray(drawn.astype(out[name].dtype))
    for name, factor in factors.items():
        out[name] = (out[name] * factor).astype(out[name].dtype)
    return out
```

```python
from contextlib import ExitStack

import numpy as np
import concourse.bass as bass
from concourse import mybir

F32 = mybir.dt.float32
BF16 = mybir.dt.bfloat16
U32 = mybir.dt.uint32
I32 = mybir.dt.int32
ALU = mybir.AluOpType
ACT = mybir.ActivationFunctionType
AX = mybir.AxisListType

P = 128
D = 1024
T = 256
TB = T // P
KD = D // P
EPS = 1e-6

H_SSD, PD, NST, GRP = 16, 64, 128, 2
CONV = 4
NCB = (D + 2 * GRP * NST) // P
H_SB, DH = 8, 64
SB_IN = H_SB * DH
H_XA, DX = 4, 128
NE, TOPK, FF = 32, 4, 1024
LIM, ALPHA = 7.0, 1.702

COL_Z, COL_XBC = 0, D
COL_DT = COL_XBC + NCB * P
COL_Q = COL_DT + H_SSD
COL_K = COL_Q + SB_IN
COL_V = COL_K + SB_IN
COL_G = COL_V + SB_IN

RING = 12
CH = 2048
SW = 512

SLOTS = 64
GE = 4
BODY = 8
NIT = NE // BODY
NPASS = T // SLOTS
GROUPS = NPASS * NE // GE
TABW = (GROUPS + 1) * GE
EXP_CH = KD + FF // P // 2


def stripes():
    s = [("xbc", "w_in", COL_XBC + SW * i, KD, "channel", "act") for i in range(3)]
    s += [("q", "w_in", COL_Q, KD, "channel", "act"), ("k", "w_in", COL_K, KD, "channel", "act"),
          ("v", "w_in", COL_V, KD, "token", "act")]
    s += [("z", "w_in", COL_Z + SW * i, KD, "token", "act") for i in range(2)]
    s += [("gate", "w_in", COL_G + SW * i, KD, "token", "act") for i in range(4)]
    s += [("xk", "w_xkv", 0, KD, "channel", "act"), ("xv", "w_xkv", H_XA * DX, KD, "token", "act")]
    for i in range(2):
        s += [("ssd_out", "w_ssd_out", SW * i, KD, "token", "dve"),
              ("sb_out", "w_sb_out", SW * i, SB_IN // P, "token", "dve")]
    s += [("out", "w_out", SW * i, KD, "token", "dve") for i in range(2)]
    s += [("xq", "w_xq", 0, KD, "channel", "act")]
    s += [("xo", "w_xo", SW * i, H_XA * DX // P, "token", "dve") for i in range(2)]
    return s


STRIPES = stripes()
FIRST = {}
for _n, _s in enumerate(STRIPES):
    FIRST.setdefault(_s[0], _n)
FIRST_CHUNK = list(np.cumsum([0] + [s[3] // 4 for s in STRIPES]))
FRONT_CH = int(FIRST_CHUNK[-1])


def emptied(n):
    if STRIPES[n][0] == "xbc":
        return "tap", 8 * (n + 1)
    return STRIPES[n][5], sum(s[5] == STRIPES[n][5] and s[0] != "xbc" for s in STRIPES[:n + 1])


def products_done(n):
    return int(FIRST_CHUNK[n + 1])


ROW_MIX, ROW_XATTN, ROW_MEM, ROW_MOE, ROW_SSD = 0, KD, 2 * KD, 3 * KD, 4 * KD
ROW_CW = 5 * KD
ROW_CB = ROW_CW + CONV * NCB
ROWS = ROW_CB + NCB


def build(nc, x, mem, g_mix, w_in, conv_w, conv_b, dt_bias, a_log, d_skip, g_ssd, w_ssd_out,
          w_sb_out, w_out, g_xattn, g_mem, w_xq, w_xkv, w_xo, g_moe, w_router, b_router,
          w_gu, b_gu, w_down, b_down, g_final, out):
    mats = {"w_in": w_in[0], "w_xkv": w_xkv[0], "w_ssd_out": w_ssd_out[0], "w_sb_out": w_sb_out[0],
            "w_out": w_out[0], "w_xq": w_xq[0], "w_xo": w_xo[0]}
    ctx = ExitStack()
    with ctx:
        def sb(name, shape, dt=F32):
            return ctx.enter_context(nc.sbuf_tensor(name, shape, dt))

        def sem(name):
            return ctx.enter_context(nc.semaphore(name))

        ring = sb("ring", [P, RING, CH])
        h = sb("h", [P, TB, D])
        xn = sb("xn", [P, TB, D])
        nT = sb("nT", [P, KD, T])
        xbuf = sb("xbuf", [P, 3136])
        xcT = sb("xcT", [P, NCB, T])
        xs = sb("xs", [P, TB, D])
        qT = sb("qT", [P, H_SB // 2, T])
        kT = sb("kT", [P, H_SB // 2, T])
        v = sb("v", [P, TB, SB_IN])
        gates = sb("gates", [P, TB, 2 * D])
        scr = sb("scr", [P, 4, 512])
        scr2 = sb("scr2", [P, 2, 512])
        cbm = sb("cbm", [P, TB * GRP, P])
        btok = sb("btok", [P, GRP, NST])
        junk = sb("junk", [P, D], BF16)
        prow = sb("prow", [ROWS, P])
        pcol = sb("pcol", [P, ROWS])
        ident = sb("ident", [P, P])
        ones = sb("ones", [P, P])
        nones = sb("nones", [P, P])
        u_incl = sb("u_incl", [P, P])
        u_strict = sb("u_strict", [P, P])
        l_strict = sb("l_strict", [P, P])
        nl_incl = sb("nl_incl", [P, P])
        identx = sb("identx", [NE, TABW])
        iota_s = sb("iota_s", [P, SLOTS])
        iota_e = sb("iota_e", [P, NE])
        w_dt = sb("w_dt", [P, KD, H_SSD])
        wr = sb("wr", [P, KD, NE])
        head_rows = sb("head_rows", [P, 3, H_SSD])
        brt = sb("brt", [P, NE])
        ss = sb("ss", [P, 16])
        epsc = sb("epsc", [P, 1])
        dt4 = sb("dt4", [P, 8, TB, H_SSD])
        lg = sb("lg", [P, TB, NE])
        top8 = sb("top8", [P, TB, 8])
        idx8 = sb("idx8", [P, TB, 8], U32)
        idxf = sb("idxf", [P, TB, TOPK])
        g4 = sb("g4", [P, TB, TOPK])
        rsm = sb("rsm", [P, 8])
        xas = sb("xas", [P, 3, 2 * H_XA])
        mask = sb("mask", [P, TB, NE])
        gate_d = sb("gate_d", [P, TB, NE])
        gateT = sb("gateT", [NE, TB, P])
        cnt_f = sb("cnt_f", [P, 1])
        cnt_i = sb("cnt_i", [P, 1], I32)

        xpad = xbuf[:, 0:NCB * (T + 3)].rearrange("p (c t) -> p c t", t=T + 3)
        z = xbuf[:, 0:TB * D].rearrange("p (b d) -> p b d", b=TB)
        xw = xbuf[:, TB * D:TB * D + D]
        merged = z
        xdt = xn
        memx = xn
        xkT = xn[:, 0, :].rearrange("p (c t) -> p c t", t=T)
        xv = xn[:, 1, :].rearrange("p (b d) -> p b d", b=TB)
        dfac = scr[:, 0:2, :]
        efac = scr[:, 2:4, :]
        s0 = scr[:, 0:2, :]
        memT = scr[:].rearrange("p a b -> p (a b)").rearrange("p (k t) -> p k t", t=T)
        gfac = scr2
        SBC = 3 * P
        xcf = xcT[:].rearrange("p c t -> p (c t)")
        sp = [xcf[:, 768 * i:768 * (i + 1)].rearrange("p (a b) -> p a b", a=2) for i in range(2)]
        wsb = [xcf[:, 768 * (2 + i):768 * (3 + i)].rearrange("p (a b) -> p a b", a=2) for i in range(2)]
        esb = xbuf[:, TB * D:TB * D + 2 * SBC].rearrange("p (a b) -> p a b", a=2)
        sbT = qT
        xqT = kT
        oT = v[:].rearrange("p b d -> p (b d)").rearrange("p (c t) -> p c t", t=T)
        hn1 = z
        hn2 = gates[:, 0, :].rearrange("p (b d) -> p b d", b=TB)
        prob = xs[:].rearrange("p b d -> p (b d)").rearrange("p (u m) -> p u m", m=T)
        probT = gates[:, 1, :].rearrange("p (h m t) -> p h m t", h=H_XA, m=TB)
        rankx, gatex = (gates[:, 1, i * TB * TABW:(i + 1) * TB * TABW].rearrange("p (b e) -> p b e", b=TB)
                        for i in range(2))
        bgu = xcf[0:NE, 0:2 * FF]
        bdn = xcf[0:NE, 2 * FF:3 * FF]
        gfin = qT[:].rearrange("p a b -> p (a b)")
        xgT = [xs[:].rearrange("p b d -> p (b d)").rearrange("p (k s) -> p k s", k=KD),
               nT]
        gl = xbuf[:, 0:512]
        ul = xbuf[:, 512:1024]
        sg = xbuf[:, 1024:1536]
        actv = xbuf[:, 1536:2048]
        actT = xbuf[:, 2048:2560].rearrange("p (c s) -> p c s", c=4)
        yb = xbuf[:, 2560:3072]
        onehot = scr[:, 0, :].rearrange("p (b e s) -> p b e s", b=TB, e=GE)
        gatehot = scr[:, 1:3, :].rearrange("p b (e u s) -> p b e u s", e=GE, u=2)
        oh4 = scr[:, 2, 0:TB * TOPK * NE].rearrange("p (b j e) -> p b j e", b=TB, j=TOPK)
        ohg = scr[:, 3, 0:TB * TOPK * NE].rearrange("p (b j e) -> p b j e", b=TB, j=TOPK)
        hotT = scr[:, 3, 2 * P:4 * P].rearrange("p (b t) -> p b t", b=TB)
        sel = scr[0:NE, 3, 0:GE * SLOTS].rearrange("p (e s) -> p e s", e=GE)

        ps = ctx.enter_context(nc.psum_tensor("ps", [P, 8, 512], F32))

        x_in, prm_in, dtw_in, mem_in, late_in, moe_in, gf_in = map(
            sem, ("x_in", "prm_in", "dtw_in", "mem_in", "late_in", "moe_in", "gf_in"))
        slot_full = [sem(f"slot_full{i}") for i in range(RING)]
        chunk_used = sem("chunk_used")
        consts = sem("consts")
        sq_done = sem("sq_done")
        rstd = sem("rstd")
        normed = sem("normed")
        tr_done, tr_out = sem("tr_done"), sem("tr_out")
        pt_done, pcol_ready = sem("pt_done"), sem("pcol_ready")
        pad_zero = sem("pad_zero")
        tap_out, conv_done, silu_done = sem("tap_out"), sem("conv_done"), sem("silu_done")
        stripe_out = {"act": sem("stripe_out_act"), "dve": sem("stripe_out_dve"), "tap": tap_out}
        dt_proj, dt_raw, dt_exp, dt_log, a_ready, da_ready = map(
            sem, ("dt_proj", "dt_raw", "dt_exp", "dt_log", "a_ready", "da_ready"))
        cs_done, cs_exp, cb_done, cbm_ready = map(sem, ("cs_done", "cs_exp", "cb_done", "cbm_ready"))
        xs_tr, xs_out, xdt_ready = sem("xs_tr"), sem("xs_out"), sem("xdt_ready")
        d_ready, seg_done, e_ready, g_ready, ydiag = map(
            sem, ("d_ready", "seg_done", "e_ready", "g_ready", "ydiag"))
        y_taken = sem("y_taken")
        xw_ready, st_done, st_out, yoff_done, yoff_taken = map(
            sem, ("xw_ready", "st_done", "st_out", "yoff_done", "yoff_taken"))
        silu_z, gate_sig, y_full = sem("silu_z"), sem("gate_sig"), sem("y_full")
        sb_lg, sb_exp, sb_log, sb_sp, sb_acc, sb_min, sb_w, sb_wm, sb_o, sb_out = map(
            sem, ("sb_lg", "sb_exp", "sb_log", "sb_sp", "sb_acc", "sb_min", "sb_w", "sb_wm", "sb_o", "sb_out"))
        xa_lg, xa_max, xa_exp, xa_prob, xa_tr, xa_trout, xa_o, xa_oout = map(
            sem, ("xa_lg", "xa_max", "xa_exp", "xa_prob", "xa_tr", "xa_trout", "xa_o", "xa_oout"))
        rt_done, rt_max, rt_exp, rt_mask, rk_done, rk_ready, gt_out = map(
            sem, ("rt_done", "rt_max", "rt_exp", "rt_mask", "rk_done", "rk_ready", "gt_out"))
        hot_ready, gathered, gather_out = sem("hot_ready"), sem("gathered"), sem("gather_out")
        gl_ready, gu_read, sg_ready, act_ready = map(
            sem, ("gl_ready", "gu_read", "sg_ready", "act_ready"))
        ht_done, ht_out, at_done, at_out, yb_ready, comb_done, y_done, yb_last, up_ready, h_full, \
            gatehot_made = map(
            sem, ("ht_done", "ht_out", "at_done", "at_out", "yb_ready", "comb_done", "y_done",
                  "yb_last", "up_ready", "h_full", "gatehot_made"))
        dve_step, act_step = sem("dve_step"), sem("act_step")
        out_sem, out_ready = sem("out_sem"), sem("out_ready")

        block = ctx.enter_context(nc.Block())

        def overflow_cond(eng):
            eng.wait_ge(rk_ready, 2)
            return eng.value_load(cnt_i[0:1, 0:1], min_val=0, max_val=T) > SLOTS

        @block.sync
        def _(sp_):
            sp_.dma_start(h[:], x[0].rearrange("(b p) d -> p b d", p=P)).then_inc(x_in, 16)
            for n, (_, mat, col, kt, _, _) in enumerate(STRIPES):
                for c in range(kt // 4):
                    m = int(FIRST_CHUNK[n]) + c
                    if m >= RING:
                        sp_.wait_ge(chunk_used, m - RING + 1)
                    src = mats[mat][c * 4 * P:(c + 1) * 4 * P, col:col + SW]
                    sp_.dma_start(ring[:, m % RING, :].rearrange("p (k n) -> p k n", k=4),
                                  src.rearrange("(k p) n -> p k n", p=P)).then_inc(slot_full[m % RING], 16)

            def expert_chunks(it, g):
                for j in range(BODY):
                    for c in range(EXP_CH):
                        m = FRONT_CH + j * EXP_CH + c
                        sp_.wait_ge(chunk_used, it * (BODY * EXP_CH) + (m - RING + 1))
                        if c < KD:
                            src = w_gu[0, bass.ds(g * BODY + j, 1), c * P:(c + 1) * P, :]
                            sp_.dma_start(ring[:, m % RING, :],
                                          src.rearrange("e p n -> (e p) n")).then_inc(slot_full[m % RING], 16)
                        else:
                            r = (c - KD) * 2 * P
                            src = w_down[0, bass.ds(g * BODY + j, 1), r:r + 2 * P, :]
                            sp_.dma_start(ring[:, m % RING, :].rearrange("p (k n) -> p k n", k=2),
                                          src.rearrange("e (k p) n -> p (e k) n", p=P)
                                          ).then_inc(slot_full[m % RING], 16)

            with sp_.Fori(0, NIT) as g:
                expert_chunks(g, g)
            with sp_.If(overflow_cond(sp_)):
                with sp_.Fori(1, NPASS) as p_:
                    with sp_.Fori(0, NIT) as g:
                        expert_chunks(p_ * NIT + g, g)
            for b in range(TB):
                sp_.wait_ge(out_ready, b + 1)
                sp_.dma_start(out[0, b * P:(b + 1) * P, :], xn[:, b, :]).then_inc(out_sem, 16)
            sp_.wait_ge(out_sem, 16 * TB)

        @block.gpsimd
        def _(pool):
            nc.gpsimd.memset(ident[:], 0.0).then_inc(consts, 1)
            nc.gpsimd.memset(ones[:], 1.0).then_inc(consts, 1)
            nc.gpsimd.memset(nones[:], -1.0).then_inc(consts, 1)
            nc.gpsimd.memset(epsc[:], EPS).then_inc(consts, 1)
            pool.wait_ge(consts, 4)
            nc.gpsimd.affine_select(out=ident[:], in_=ident[:], compare_op=ALU.not_equal, fill=1.0, base=0,
                                    pattern=[[-1, P]], channel_multiplier=1).then_inc(consts, 1)
            for row, vec, n in ((ROW_MIX, g_mix, KD), (ROW_XATTN, g_xattn, KD), (ROW_MEM, g_mem, KD),
                                (ROW_MOE, g_moe, KD), (ROW_SSD, g_ssd, KD), (ROW_CB, conv_b, NCB)):
                pool.dma_start(prow[row:row + n, :], vec[0].rearrange("(k p) -> k p", p=P)).then_inc(prm_in, 16)
            pool.dma_start(prow[ROW_CW:ROW_CB, :],
                           conv_w[0].rearrange("j (k p) -> (j k) p", p=P)).then_inc(prm_in, 16)
            pool.dma_start(w_dt[:], w_in[0, :, COL_DT:COL_Q].rearrange("(k p) n -> p k n", p=P)).then_inc(dtw_in, 16)
            for i, vec in enumerate((dt_bias, a_log, d_skip)):
                pool.dma_start(head_rows[:, i, :], vec[0].partition_broadcast(P)).then_inc(dtw_in, 16)
            for dst, src, pat, cm, op in ((u_incl, ones, 1, -1, ALU.is_ge), (u_strict, ones, 1, -1, ALU.is_gt),
                                          (l_strict, ones, -1, 1, ALU.is_gt), (nl_incl, nones, -1, 1, ALU.is_ge)):
                nc.gpsimd.affine_select(out=dst[:], in_=src[:], compare_op=op, fill=0.0, base=0,
                                        pattern=[[pat, P]], channel_multiplier=cm).then_inc(consts, 1)
            nc.gpsimd.iota(iota_s[:], pattern=[[1, SLOTS]], base=0, channel_multiplier=0,
                           allow_small_or_imprecise_dtypes=True).then_inc(consts, 1)
            nc.gpsimd.iota(iota_e[:], pattern=[[1, NE]], base=0, channel_multiplier=0,
                           allow_small_or_imprecise_dtypes=True).then_inc(consts, 1)
            pool.wait_ge(consts, 5)
            for c in range(0, TABW, NE):
                w = min(NE, TABW - c)
                nc.gpsimd.tensor_copy(identx[:, c:c + w], ident[0:NE, 0:w]).then_inc(consts, 1)
            pool.dma_start(wr[:], w_router[0].rearrange("(k p) n -> p k n", p=P)).then_inc(late_in, 16)
            pool.dma_start(brt[:], b_router[0].partition_broadcast(P)).then_inc(late_in, 16)
            pool.wait_ge(ydiag, 8)
            pool.wait_ge(xw_ready, 1)
            pool.dma_start(memx[:], mem[0].rearrange("(b p) d -> p b d", p=P)).then_inc(mem_in, 16)
            pool.wait_ge(sb_o, 4)
            pool.dma_start(bgu, b_gu[0]).then_inc(moe_in, 16)
            pool.dma_start(bdn, b_down[0]).then_inc(moe_in, 16)
            pool.wait_ge(chunk_used, products_done(FIRST["sb_out"] + 2))
            pool.dma_start(gfin, g_final.partition_broadcast(P)).then_inc(gf_in, 16)

        N_CONST = 5 + 4 + 2 + -(-TABW // NE)

        @block.tensor
        def _(pe):
            mm = nc.tensor.matmul

            def chunk(m):
                pe.wait_ge(slot_full[m % RING], 16 * (m // RING + 1))
                return ring[:, m % RING, :].rearrange("p (k n) -> p k n", k=4)

            def stripe(n, src):
                _, _, _, kt, layout, _ = STRIPES[n]
                b0 = 2 * (n % 2)
                if n >= 2:
                    eng, count = emptied(n - 2)
                    pe.wait_ge(stripe_out[eng], count)
                m0 = int(FIRST_CHUNK[n])
                if layout == "channel":
                    w = [chunk(m0), chunk(m0 + 1)]
                    for cb in range(4):
                        for k in range(kt):
                            i = mm(ps[:, b0 + cb // 2, (cb % 2) * T:(cb % 2 + 1) * T],
                                   w[k // 4][:, k % 4, cb * P:(cb + 1) * P], src[:, k, :],
                                   start=(k == 0), stop=(k == kt - 1))
                            if cb == 3 and k % 4 == 3:
                                i.then_inc(chunk_used, 1)
                else:
                    for c in range(kt // 4):
                        w = chunk(m0 + c)
                        for b in range(TB):
                            for k in range(4):
                                i = mm(ps[:, b0 + b, :], src[:, 4 * c + k, b * P:(b + 1) * P], w[:, k, :],
                                       start=(c == 0 and k == 0), stop=(4 * c + k == kt - 1))
                        i.then_inc(chunk_used, 1)

            def transposes(n, src):
                for b in range(TB):
                    for half in range(2):
                        for k in range(4):
                            i = nc.tensor.transpose(ps[:, 4 + 2 * b + half, k * P:(k + 1) * P],
                                                    src[:, b, (4 * half + k) * P:(4 * half + k + 1) * P], ident[:])
                        i.then_inc(tr_done, 1)

            pe.wait_ge(prm_in, 16 * 7)
            pe.wait_ge(consts, 9)
            nc.tensor.transpose(ps[:, 3, 0:ROWS], prow[:], ident[0:ROWS, 0:ROWS]).then_inc(pt_done, 1)
            pe.wait_ge(normed, TB)
            transposes(0, xn)
            pe.wait_ge(tr_out, 4)
            for n in range(3):
                stripe(n, nT)
            pe.wait_ge(dtw_in, 64)
            for b in range(TB):
                for k in range(KD):
                    i = mm(ps[:, 4, b * H_SSD:(b + 1) * H_SSD], nT[:, k, b * P:(b + 1) * P], w_dt[:, k, :],
                           start=(k == 0), stop=(k == KD - 1))
            i.then_inc(dt_proj, 1)
            stripe(FIRST["q"], nT)
            pe.wait_ge(da_ready, 1)
            da = dt4[:, 5, :, :].rearrange("p b h -> p (b h)")
            mm(ps[:, 4, 32:64], u_incl[:], da, start=True, stop=True)
            mm(ps[:, 4, 64:96], l_strict[:], da, start=True, stop=True).then_inc(cs_done, 1)
            stripe(FIRST["k"], nT)
            pe.wait_ge(silu_done, 3)
            for b in range(TB):
                for g in range(GRP):
                    i = mm(ps[:, 5, (b * GRP + g) * P:(b * GRP + g + 1) * P], xcT[:, 8 + g, b * P:(b + 1) * P],
                           xcT[:, 10 + g, b * P:(b + 1) * P], start=True, stop=True)
            i.then_inc(cb_done, 1)

            def xs_transposes(half):
                if half:
                    pe.wait_ge(xs_out, 2)
                for b in range(TB):
                    for k in range(4):
                        i = nc.tensor.transpose(ps[:, 6 + b, k * P:(k + 1) * P],
                                                xcT[:, 4 * half + k, b * P:(b + 1) * P], ident[:])
                i.then_inc(xs_tr, 1)

            xs_transposes(0)
            stripe(FIRST["v"], nT)
            xs_transposes(1)
            pe.wait_ge(cs_exp, 1)
            for g in range(GRP):
                i = nc.tensor.transpose(ps[:, 4, g * P:(g + 1) * P], xcT[:, 8 + g, 0:P], ident[:])
            i.then_inc(xs_tr, 1)

            def seg(j):
                pe.wait_ge(d_ready, j + 1)
                if j >= 2:
                    pe.wait_ge(e_ready, j - 1)
                else:
                    pe.wait_ge(xs_out, 4)
                mm(ps[:, 6 + j % 2, :], l_strict[:], dfac[:, j % 2, :], start=True, stop=True).then_inc(seg_done, 1)

            def y_diag(j):
                pe.wait_ge(g_ready, j + 1)
                b, q = j // 4, j % 4
                if j == 0:
                    pe.wait_ge(xdt_ready, 1)
                    pe.wait_ge(xs_out, 5)
                if b == 1 and q % 2 == 0:
                    pe.wait_ge(y_taken, q // 2 + 1)
                for i4 in range(4):
                    hd = 4 * q + i4
                    i = mm(ps[:, 4 + q // 2, (hd % 8) * PD:(hd % 8 + 1) * PD],
                           gfac[:, j % 2, i4 * P:(i4 + 1) * P], xdt[:, b, hd * PD:(hd + 1) * PD],
                           start=True, stop=True)
                i.then_inc(ydiag, 1)

            seg(0)
            seg(1)
            stripe(FIRST["z"], nT)
            for r in range(1, 5):
                y_diag(2 * r - 2)
                y_diag(2 * r - 1)
                if r < 4:
                    seg(2 * r)
                    seg(2 * r + 1)
                stripe(FIRST["z"] + r, nT)
            pe.wait_ge(xw_ready, 1)
            pe.wait_ge(e_ready, 8)
            for g in range(GRP):
                i = mm(ps[:, 6 + g, :], btok[:, g, :], xw[:, g * 512:(g + 1) * 512], start=True, stop=True)
            i.then_inc(st_done, 1)
            stripe(FIRST["gate"] + 3, nT)
            pe.wait_ge(st_out, 1)
            for g in range(GRP):
                i = mm(ps[:, 6 + g, :], xcT[:, 10 + g, P:2 * P], s0[:, g, :], start=True, stop=True)
            i.then_inc(yoff_done, 1)

            def sb_logits(i):
                b0 = 4 + 2 * (i % 2)
                if i == 0:
                    pe.wait_ge(y_taken, 4)
                elif i == 1:
                    pe.wait_ge(yoff_taken, 1)
                else:
                    pe.wait_ge(sb_out, i - 1)
                for e in range(2):
                    r = slice(64 * e, 64 * e + 64)
                    mm(ps[:, b0 + e, 0:T], kT[r, i, 0:P], qT[r, i, :], start=True, stop=False,
                       skip_group_check=True)
                    j = mm(ps[:, b0 + e, T:SBC], kT[r, i, P:T], qT[r, i, P:T], start=False, stop=False,
                           skip_group_check=True)
                j.then_inc(sb_lg, 1)

            def sb_stay(i):
                b0 = 4 + 2 * (i % 2)
                pe.wait_ge(sb_sp, i + 1)
                for e in range(2):
                    s = sp[i % 2][:, e, :]
                    mm(ps[:, b0 + e, 0:T], nl_incl[:], s[:, 0:T], start=False, stop=False, skip_group_check=True)
                    mm(ps[:, b0 + e, T:SBC], nl_incl[:], s[:, T:SBC], start=False, stop=False,
                       skip_group_check=True)
                    j = mm(ps[:, b0 + e, P:T], nones[:], s[:, T:SBC], start=False, stop=True,
                           skip_group_check=True)
                j.then_inc(sb_acc, 1)

            def sb_values(i):
                b0 = 4 + 2 * (i % 2)
                pe.wait_ge(sb_wm, i + 1)
                for e in range(2):
                    hd = 2 * i + e
                    o = ps[64 * e:64 * e + 64, b0, :]
                    mm(o[:, 0:T], v[:, 0, hd * DH:(hd + 1) * DH], wsb[i % 2][:, e, 0:T], start=True, stop=False,
                       skip_group_check=True)
                    j = mm(o[:, P:T], v[:, 1, hd * DH:(hd + 1) * DH], wsb[i % 2][:, e, T:SBC], start=False,
                           stop=True, skip_group_check=True)
                j.then_inc(sb_o, 1)

            sb_logits(0)
            sb_logits(1)
            sb_stay(0)
            sb_stay(1)
            sb_values(0)
            sb_logits(2)
            sb_values(1)
            sb_logits(3)
            sb_stay(2)
            sb_stay(3)
            sb_values(2)
            sb_values(3)
            pe.wait_ge(normed, 2 * TB)
            pe.wait_ge(sb_out, 4)
            transposes(1, memx)
            pe.wait_ge(tr_out, 8)
            stripe(FIRST["xk"], memT)
            stripe(FIRST["xv"], memT)
            pe.wait_ge(normed, 3 * TB)
            transposes(2, xs)
            pe.wait_ge(tr_out, 12)
            for n in range(2):
                stripe(FIRST["ssd_out"] + 2 * n, nT)
                stripe(FIRST["sb_out"] + 2 * n, sbT)
            pe.wait_ge(normed, 4 * TB)
            transposes(3, merged)
            pe.wait_ge(tr_out, 16)
            for n in range(2):
                stripe(FIRST["out"] + n, nT)
            pe.wait_ge(normed, 5 * TB)
            transposes(4, hn1)
            pe.wait_ge(tr_out, 20)
            stripe(FIRST["xq"], nT)
            pe.wait_ge(stripe_out["act"], emptied(FIRST["xq"])[1])
            for hd in range(H_XA):
                for b in range(TB):
                    i = mm(ps[:, 4 + hd, b * T:(b + 1) * T], xqT[:, hd, b * P:(b + 1) * P], xkT[:, hd, :],
                           start=True, stop=True)
                i.then_inc(xa_lg, 1)
            for hd in range(H_XA):
                pe.wait_ge(xa_prob, hd + 1)
                for mb in range(TB):
                    for b in range(TB):
                        i = nc.tensor.transpose(ps[:, 4 + hd, mb * T + b * P:mb * T + (b + 1) * P],
                                                prob[:, 2 * hd + b, mb * P:(mb + 1) * P], ident[:])
                i.then_inc(xa_tr, 1)
            for hd in range(H_XA):
                pe.wait_ge(xa_trout, hd + 1)
                if hd == 0:
                    pe.wait_ge(xa_trout, 2)
                for mb in range(TB):
                    i = mm(ps[:, 4 + hd // 2, (hd % 2) * T:(hd % 2 + 1) * T], xv[:, mb, hd * DX:(hd + 1) * DX],
                           probT[:, hd, mb, :], start=(mb == 0), stop=(mb == TB - 1))
                if hd % 2:
                    i.then_inc(xa_o, 1)
            pe.wait_ge(xa_oout, 2)
            for n in range(2):
                stripe(FIRST["xo"] + n, oT)
            pe.wait_ge(normed, 6 * TB)
            transposes(5, hn2)
            pe.wait_ge(tr_out, 24)
            pe.wait_ge(late_in, 32)
            for b in range(TB):
                for k in range(KD):
                    i = mm(ps[:, 4, b * NE:(b + 1) * NE], nT[:, k, b * P:(b + 1) * P], wr[:, k, :],
                           start=(k == 0), stop=(k == KD - 1))
            i.then_inc(rt_done, 1)
            pe.wait_ge(rt_mask, 2)
            mm(ps[:, 5, 0:NE], u_strict[:], mask[:, 0, :], start=True, stop=True)
            mm(ps[:, 5, NE:2 * NE], ones[:], mask[:, 0, :], start=True, stop=False)
            mm(ps[:, 5, NE:2 * NE], u_strict[:], mask[:, 1, :], start=False, stop=True)
            mm(ps[:, 5, 2 * NE:3 * NE], ones[:], mask[:, 0, :], start=True, stop=False)
            mm(ps[:, 5, 2 * NE:3 * NE], ones[:], mask[:, 1, :], start=False, stop=True)
            for b in range(TB):
                i = nc.tensor.transpose(ps[0:NE, 6, b * P:(b + 1) * P], gate_d[:, b, :], ident[:])
            i.then_inc(rk_done, 1)
            pe.wait_ge(gt_out, 1)
            pe.wait_ge(moe_in, 32)
            pe.wait_ge(stripe_out["dve"], emptied(FIRST["xo"] + 1)[1])
            for b in range(TB):
                for half in range(2):
                    mm(ps[:, 2 * b + half, :], gateT[:, b, :], bdn[:, half * 512:(half + 1) * 512],
                       start=True, stop=False, skip_group_check=True)

            def gather(k0):
                for k in range(2):
                    for b in range(TB):
                        i = mm(ps[:, 7, k * T:(k + 1) * T], hn2[:, b, (k0 + k) * P:(k0 + k + 1) * P],
                               onehot[:, b, :, :].rearrange("p e s -> p (e s)"), start=(b == 0), stop=(b == 1))
                i.then_inc(gathered, 1)

            pe.wait_ge(hot_ready, 1)
            for k0 in range(0, KD, 2):
                if k0:
                    pe.wait_ge(gather_out, k0 // 2)
                gather(k0)

            def combine(done=comb_done):
                for b in range(TB):
                    for half in range(2):
                        r = slice(64 * half, 64 * half + 64)
                        i = mm(ps[:, 2 * b + half, :], hotT[r, b, :], yb[r, :], start=False, stop=False,
                               skip_group_check=True)
                i.then_inc(done, 1)

            def experts(it):
                for j in range(BODY):
                    n = it * BODY + j
                    xg = xgT[j // GE]
                    if j % GE == 0:
                        pe.wait_ge(hot_ready, it * 2 + (j // GE + 2))
                        pe.wait_ge(gather_out, it * 8 + (4 * (j // GE) + 4))
                    for q in range(2):
                        for half in range(2):
                            mm(ps[64 * half:64 * half + 64, 4 + q, :], sel[:, j % GE, :],
                               bgu[:, q * FF + half * 512:q * FF + half * 512 + 512],
                               start=True, stop=False, skip_group_check=True)
                    for k in range(KD):
                        m = FRONT_CH + j * EXP_CH + k
                        pe.wait_ge(slot_full[m % RING], it * (16 * BODY * EXP_CH // RING) + 16 * (m // RING + 1))
                        w = ring[:, m % RING, :]
                        for q in range(2):
                            for half in range(2):
                                i = mm(ps[64 * half:64 * half + 64, 4 + q, :],
                                       xg[:, k, (j % GE) * SLOTS:(j % GE + 1) * SLOTS],
                                       w[:, q * FF + half * 512:q * FF + half * 512 + 512],
                                       start=False, stop=(k == KD - 1), skip_group_check=True)
                        i.then_inc(chunk_used, 1)
                    pe.wait_ge(yb_ready, n + 1)
                    combine()
                    gather(2 * (j % GE))
                    for b in range(TB):
                        i = nc.tensor.transpose(ps[:, 6, b * P:(b + 1) * P],
                                                gatehot[:, b, j % GE].rearrange("p u s -> p (u s)"),
                                                ident[:])
                    i.then_inc(ht_done, 1)
                    pe.wait_ge(gather_out, it * 8 + (j + 5))
                    pe.wait_ge(act_ready, n + 1)
                    for c in range(4):
                        i = nc.tensor.transpose(ps[:, 7, c * P:(c + 1) * P], actv[:, c * P:(c + 1) * P], ident[:])
                    i.then_inc(at_done, 1)
                    pe.wait_ge(ht_out, n + 1)
                    pe.wait_ge(at_out, n + 1)
                    for k in range(FF // P):
                        m = FRONT_CH + j * EXP_CH + KD + k // 2
                        if k % 2 == 0:
                            pe.wait_ge(slot_full[m % RING], it * (16 * BODY * EXP_CH // RING) + 16 * (m // RING + 1))
                        w = ring[:, m % RING, :].rearrange("p (k n) -> p k n", k=2)
                        fh, c = k // 4, k % 4
                        for half in range(2):
                            i = mm(ps[64 * half:64 * half + 64, 6, :], actT[:, c, fh * 64:fh * 64 + 64],
                                   w[:, k % 2, half * 512:(half + 1) * 512],
                                   start=(k == 0), stop=(k == FF // P - 1), skip_group_check=True)
                        if k % 2:
                            i.then_inc(chunk_used, 1)

            with pe.Fori(0, NIT) as g:
                experts(g)
            with pe.If(overflow_cond(pe)):
                with pe.Fori(1, NPASS) as p_:
                    with pe.Fori(0, NIT) as g:
                        experts(p_ * NIT + g)
            pe.wait_ge(yb_last, 1)
            combine(y_done)

        @block.scalar
        def _(act):
            af = nc.scalar.activation
            count = [0]

            def step(ins):
                count[0] += 1
                ins.then_inc(act_step, 1)
                act.wait_ge(act_step, count[0])

            def root(n, c0, cols, width):
                act.wait_ge(sq_done, n)
                s = ss[:, c0:c0 + cols]
                step(af(s, s, ACT.Ln, bias=epsc[:], scale=1.0 / width))
                af(s, s, ACT.Exp, scale=-0.5).then_inc(rstd, 1)

            sq = [0]

            def squares(src, c0):
                for b in range(TB):
                    if sq[0]:
                        act.wait_ge(sq_done, sq[0])
                    sq[0] += 1
                    af(junk[:], src[:, b, :], ACT.Square, accum_out=ss[:, c0 + b:c0 + b + 1]).then_inc(sq_done, 1)

            def empty(n, func=ACT.Copy, scale=1.0):
                name, _, _, _, layout, _ = STRIPES[n]
                b0, i = 2 * (n % 2), n - FIRST[name]
                act.wait_ge(chunk_used, products_done(n))
                src = ps[:, b0:b0 + 2, :]
                if layout == "channel":
                    src = src.rearrange("p b (c t) -> p (b c) t", t=T)
                    dst = {"q": qT, "k": kT, "xk": xkT, "xq": xqT}[name][:, 0:4, :]
                else:
                    dst = {"v": lambda: v[:, :, :], "xv": lambda: xv,
                           "z": lambda: z[:, :, i * SW:(i + 1) * SW],
                           "gate": lambda: gates[:, :, i * SW:(i + 1) * SW]}[name]()
                return af(dst, src, func, scale=scale).then_inc(stripe_out["act"], 1)

            act.wait_ge(consts, 5)
            act.wait_ge(x_in, 16)
            squares(h, 0)
            root(2, 0, 2, D)
            act.wait_ge(pad_zero, 1)
            act.wait_ge(pcol_ready, 1)
            for n in range(3):
                act.wait_ge(chunk_used, products_done(n))
                for cb in range(4):
                    c = 4 * n + cb
                    src = ps[:, 2 * (n % 2) + cb // 2, (cb % 2) * T:(cb % 2 + 1) * T]
                    af(xpad[:, c, 3:], src, ACT.Copy).then_inc(tap_out, 1)
                    af(xcT[:, c, :], src, ACT.Identity, bias=pcol[:, ROW_CB + c:ROW_CB + c + 1],
                       scale=pcol[:, ROW_CW + 3 * NCB + c:ROW_CW + 3 * NCB + c + 1]).then_inc(tap_out, 1)
            act.wait_ge(dtw_in, 64)
            act.wait_ge(dt_raw, 2)
            af(dt4[:, 2], dt4[:, 1], ACT.Exp, scale=-1.0).then_inc(dt_exp, 1)
            act.wait_ge(dt_exp, 1)
            af(dt4[:, 3], dt4[:, 2], ACT.Ln, bias=1.0).then_inc(dt_log, 1)
            af(head_rows[:, 1, :], head_rows[:, 1, :], ACT.Exp).then_inc(a_ready, 1)
            for n in range(3):
                act.wait_ge(conv_done, 4 * n + 4)
                af(xcT[:, 4 * n:4 * n + 4, :], xcT[:, 4 * n:4 * n + 4, :], ACT.Silu).then_inc(silu_done, 1)
            empty(FIRST["q"], scale=DH ** -0.5)
            act.wait_ge(cs_done, 1)
            af(dt4[:, 6:8].rearrange("p a b h -> p (a b h)"), ps[:, 4, 32:96], ACT.Exp).then_inc(cs_exp, 1)
            empty(FIRST["k"])

            def xs_copy(half):
                act.wait_ge(xs_tr, half + 1)
                for b in range(TB):
                    af(xs[:, b, half * 512:(half + 1) * 512], ps[:, 6 + b, :], ACT.Copy).then_inc(xs_out, 1)

            xs_copy(0)
            empty(FIRST["v"])
            xs_copy(1)
            act.wait_ge(xs_tr, 3)
            af(btok[:].rearrange("p g n -> p (g n)"), ps[:, 4, 0:GRP * NST], ACT.Copy).then_inc(xs_out, 1)

            def seg_exp(j):
                act.wait_ge(seg_done, j + 1)
                if j >= 2:
                    act.wait_ge(g_ready, j - 1)
                af(efac[:, j % 2, :], ps[:, 6 + j % 2, :], ACT.Exp).then_inc(e_ready, 1)

            seg_exp(0)
            seg_exp(1)
            empty(FIRST["z"])
            for r in range(1, 5):
                if r < 4:
                    seg_exp(2 * r)
                    seg_exp(2 * r + 1)
                empty(FIRST["z"] + r)
            act.wait_ge(st_done, 1)
            act.wait_ge(seg_done, 8)
            af(s0, ps[:, 6:8, :], ACT.Copy).then_inc(st_out, 1)
            empty(FIRST["gate"] + 3)

            def sb_softplus(i):
                b0 = 4 + 2 * (i % 2)
                act.wait_ge(sb_lg, i + 1)
                if i == 0:
                    act.wait_ge(xw_ready, 1)
                    act.wait_ge(st_done, 1)
                if i >= 1:
                    act.wait_ge(sb_sp, i)
                step(af(esb, ps[:, b0:b0 + 2, 0:SBC], ACT.Abs))
                step(af(esb, esb, ACT.Exp, scale=-1.0))
                af(esb, esb, ACT.Ln, bias=1.0).then_inc(sb_log, 1)

            def sb_weights(i):
                act.wait_ge(sb_min, i + 1)
                af(wsb[i % 2], wsb[i % 2], ACT.Exp).then_inc(sb_w, 1)

            sb_softplus(0)
            sb_softplus(1)
            sb_weights(0)
            sb_weights(1)
            sb_softplus(2)
            sb_softplus(3)
            sb_weights(2)
            sb_weights(3)
            act.wait_ge(stripe_out["act"], emptied(FIRST["gate"] + 3)[1])
            af(z, z, ACT.Silu).then_inc(silu_z, 1)
            for half in range(2):
                af(gates[:, half, :], gates[:, half, :], ACT.Sigmoid).then_inc(gate_sig, 1)
            act.wait_ge(mem_in, 16)
            squares(memx, 2)
            root(4, 2, 2, D)
            act.wait_ge(y_full, 1)
            for b in range(TB):
                for g in range(GRP):
                    act.wait_ge(sq_done, sq[0])
                    sq[0] += 1
                    af(junk[:, 0:512], xs[:, b, g * 512:(g + 1) * 512], ACT.Square,
                       accum_out=ss[:, 4 + 2 * b + g:5 + 2 * b + g]).then_inc(sq_done, 1)
            root(8, 4, 4, D // GRP)
            empty(FIRST["xk"])
            empty(FIRST["xv"])
            act.wait_ge(stripe_out["dve"], emptied(FIRST["out"] + 1)[1])
            squares(h, 8)
            root(10, 8, 2, D)
            empty(FIRST["xq"], scale=DX ** -0.5)
            for hd in range(H_XA):
                act.wait_ge(xa_max, hd + 1)
                for b in range(TB):
                    u = 2 * hd + b
                    af(prob[:, u, :], ps[:, 4 + hd, b * T:(b + 1) * T], ACT.Exp, bias=xas[:, 0, u:u + 1],
                       accum_out=xas[:, 1, u:u + 1]).then_inc(xa_exp, 1)
            for hd in range(H_XA):
                act.wait_ge(xa_tr, hd + 1)
                af(probT[:, hd].rearrange("p m t -> p (m t)"), ps[:, 4 + hd, :], ACT.Copy).then_inc(xa_trout, 1)
            for i in range(2):
                act.wait_ge(xa_o, i + 1)
                af(oT[:, 2 * i:2 * i + 2, :].rearrange("p h t -> p (h t)"), ps[:, 4 + i, :],
                   ACT.Copy).then_inc(xa_oout, 1)
            act.wait_ge(stripe_out["dve"], emptied(FIRST["xo"] + 1)[1])
            squares(h, 10)
            root(12, 10, 2, D)
            act.wait_ge(rt_max, 1)
            for b in range(TB):
                af(g4[:, b, :], top8[:, b, 0:TOPK], ACT.Exp, bias=rsm[:, b:b + 1],
                   accum_out=rsm[:, 2 + b:3 + b]).then_inc(rt_exp, 1)
            act.wait_ge(rk_done, 1)
            af(gateT[:].rearrange("p b t -> p (b t)"), ps[0:NE, 6, 0:T], ACT.Copy).then_inc(gt_out, 1)

            def experts(it):
                for j in range(BODY):
                    n = it * BODY + j
                    act.wait_ge(gl_ready, n + 1)
                    af(sg, gl, ACT.Sigmoid, scale=ALPHA).then_inc(sg_ready, 1)
                    act.wait_ge(ht_done, n + 1)
                    af(hotT.rearrange("p b t -> p (b t)"), ps[:, 6, 0:2 * P], ACT.Copy).then_inc(ht_out, 1)
                    act.wait_ge(at_done, n + 1)
                    af(actT.rearrange("p c s -> p (c s)"), ps[:, 7, :], ACT.Copy).then_inc(at_out, 1)

            with act.Fori(0, NIT) as g:
                experts(g)
            with act.If(overflow_cond(act)):
                with act.Fori(1, NPASS) as p_:
                    with act.Fori(0, NIT) as g:
                        experts(p_ * NIT + g)
            act.wait_ge(h_full, 1)
            squares(h, 12)
            root(14, 12, 2, D)

        @block.vector
        def _(dve):
            V = nc.vector
            count = [0]

            def step(ins):
                count[0] += 1
                ins.then_inc(dve_step, 1)
                dve.wait_ge(dve_step, count[0])

            def normalise(n, dst, src, c0):
                for b in range(TB):
                    V.tensor_scalar(dst[:, b, :], src[:, b, :], ss[:, c0 + b:c0 + b + 1], None,
                                    ALU.mult).then_inc(normed, 1)

            def take_transposed(n, dst, row):
                for b in range(TB):
                    for half in range(2):
                        dve.wait_ge(tr_done, 4 * n + 2 * b + half + 1)
                        src = ps[:, 4 + 2 * b + half, :].rearrange("p (k t) -> p k t", k=4)
                        d = dst[:, 4 * half:4 * half + 4, b * P:(b + 1) * P]
                        if row is None:
                            V.tensor_copy(d, src).then_inc(tr_out, 1)
                        else:
                            g = pcol[:, row + 4 * half:row + 4 * half + 4].unsqueeze(2).broadcast_to([P, 4, P])
                            V.tensor_tensor(d, src, g, ALU.mult).then_inc(tr_out, 1)

            V.memset(xpad[:, :, 0:3], 0.0).then_inc(pad_zero, 1)
            dve.wait_ge(rstd, 1)
            normalise(0, xn, h, 0)
            dve.wait_ge(pt_done, 1)
            V.tensor_copy(pcol[:], ps[:, 3, 0:ROWS]).then_inc(pcol_ready, 1)
            dve.wait_ge(pcol_ready, 1)
            take_transposed(0, nT, ROW_MIX)

            def convolve(c):
                for tap in range(3):
                    if tap == 0:
                        dve.wait_ge(tap_out, 2 * c + 2)
                    i = V.scalar_tensor_tensor(out=xcT[:, c, :], in0=xpad[:, c, tap:tap + T],
                                               scalar=pcol[:, ROW_CW + tap * NCB + c:ROW_CW + tap * NCB + c + 1],
                                               in1=xcT[:, c, :], op0=ALU.mult, op1=ALU.add)
                    if tap < 2:
                        step(i)
                    else:
                        i.then_inc(conv_done, 1)

            for c in range(NCB):
                convolve(c)
            dve.wait_ge(dt_proj, 1)
            dve.wait_ge(dtw_in, 64)

            def per_head(i):
                return head_rows[:, i, :].unsqueeze(1).broadcast_to([P, TB, H_SSD])

            V.tensor_tensor(dt4[:, 0], ps[:, 4, 0:32].rearrange("p (b h) -> p b h", b=TB), per_head(0),
                            ALU.add).then_inc(dt_raw, 1)
            dve.wait_ge(dt_raw, 1)
            V.scalar_tensor_tensor(out=dt4[:, 1], in0=dt4[:, 0], scalar=-1.0, in1=dt4[:, 0],
                                   op0=ALU.mult, op1=ALU.max).then_inc(dt_raw, 1)
            dve.wait_ge(dt_log, 1)
            step(V.scalar_tensor_tensor(out=dt4[:, 4], in0=dt4[:, 0], scalar=0.0, in1=dt4[:, 3],
                                        op0=ALU.max, op1=ALU.add))
            dve.wait_ge(a_ready, 1)
            V.scalar_tensor_tensor(out=dt4[:, 5], in0=dt4[:, 4], scalar=-1.0, in1=per_head(1),
                                   op0=ALU.mult, op1=ALU.mult).then_inc(da_ready, 1)
            dve.wait_ge(da_ready, 1)

            def d_factor(j):
                if j >= 2:
                    dve.wait_ge(seg_done, j - 1)
                b, q = j // 4, j % 4
                V.tensor_tensor(dfac[:, j % 2, :].rearrange("p (h l) -> p h l", h=4),
                                u_incl[:].unsqueeze(1).broadcast_to([P, 4, P]),
                                dt4[:, 5, b, 4 * q:4 * q + 4].unsqueeze(2).broadcast_to([P, 4, P]),
                                ALU.mult).then_inc(d_ready, 1)

            def g_factor(j):
                dve.wait_ge(e_ready, j + 1)
                if j >= 2:
                    dve.wait_ge(ydiag, j - 1)
                b, q = j // 4, j % 4
                V.tensor_tensor(gfac[:, j % 2, :].rearrange("p (h l) -> p h l", h=4),
                                efac[:, j % 2, :].rearrange("p (h l) -> p h l", h=4),
                                cbm[:, b * GRP + q // 2, :].unsqueeze(1).broadcast_to([P, 4, P]),
                                ALU.mult).then_inc(g_ready, 1)

            dve.wait_ge(consts, 9)
            d_factor(0)
            d_factor(1)
            dve.wait_ge(cb_done, 1)
            V.tensor_tensor(cbm[:], ps[:, 5, :].rearrange("p (c l) -> p c l", c=4),
                            u_incl[:].unsqueeze(1).broadcast_to([P, 4, P]), ALU.mult).then_inc(cbm_ready, 1)
            dve.wait_ge(cbm_ready, 1)
            dve.wait_ge(xs_out, 4)

            def heads(t, width=PD):
                return t.unsqueeze(2).broadcast_to([P, H_SSD, width])

            for b in range(TB):
                i = V.tensor_tensor(xdt[:, b, :].rearrange("p (h d) -> p h d", d=PD),
                                    xs[:, b, :].rearrange("p (h d) -> p h d", d=PD), heads(dt4[:, 4, b, :]), ALU.mult)
                if b == 0:
                    step(i)
                else:
                    i.then_inc(xdt_ready, 1)
            for b in range(TB):
                xb = xs[:, b, :].rearrange("p (h d) -> p h d", d=PD)
                step(V.tensor_tensor(xb, xb, heads(head_rows[:, 2, :]), ALU.mult))

            def take_y(b, half):
                dve.wait_ge(ydiag, 4 * b + 2 * half + 2)
                yy = xs[:, b, half * 512:(half + 1) * 512]
                V.tensor_tensor(yy, ps[:, 4 + half, :], yy, ALU.add).then_inc(y_taken, 1)

            g_factor(0)
            g_factor(1)
            d_factor(2)
            d_factor(3)
            dve.wait_ge(cs_exp, 1)
            V.tensor_tensor(xw.rearrange("p (h d) -> p h d", d=PD), xdt[:, 0, :].rearrange("p (h d) -> p h d", d=PD),
                            heads(dt4[:, 7, 0, :]), ALU.mult).then_inc(xw_ready, 1)
            take_y(0, 0)
            g_factor(2)
            g_factor(3)
            d_factor(4)
            d_factor(5)
            take_y(0, 1)
            g_factor(4)
            g_factor(5)
            d_factor(6)
            d_factor(7)
            take_y(1, 0)
            g_factor(6)
            g_factor(7)
            take_y(1, 1)
            dve.wait_ge(yoff_done, 1)
            dve.wait_ge(ydiag, 8)
            yo = gfac[:].rearrange("p a b -> p (a b)").rearrange("p (h d) -> p h d", d=PD)
            V.tensor_tensor(yo, ps[:, 6:8, :].rearrange("p a (h d) -> p (a h) d", d=PD), heads(dt4[:, 6, 1, :]),
                            ALU.mult).then_inc(yoff_taken, 1)
            dve.wait_ge(yoff_taken, 1)
            dve.wait_ge(y_taken, 4)
            step(V.tensor_tensor(xs[:, 1, :], xs[:, 1, :], gfac[:].rearrange("p a b -> p (a b)"), ALU.add))

            def diag(t):
                return [t[:, e, :].rearrange("p (c t) -> p c t", t=P)[:, 0:3:2, :] for e in range(2)]

            keep = u_strict[:].unsqueeze(1).broadcast_to([P, 2, P])

            def sb_softplus(i):
                dve.wait_ge(sb_log, i + 1)
                if i >= 2:
                    dve.wait_ge(sb_acc, i - 1)
                step(V.scalar_tensor_tensor(out=sp[i % 2], in0=ps[:, 4 + 2 * (i % 2):6 + 2 * (i % 2), 0:SBC],
                                            scalar=0.0, in1=esb, op0=ALU.max, op1=ALU.add))
                a, b = diag(sp[i % 2])
                step(V.tensor_tensor(a, a, keep, ALU.mult))
                V.tensor_tensor(b, b, keep, ALU.mult).then_inc(sb_sp, 1)

            def sb_clip(i):
                dve.wait_ge(sb_acc, i + 1)
                if i >= 2:
                    dve.wait_ge(sb_o, i - 1)
                V.tensor_scalar(wsb[i % 2], ps[:, 4 + 2 * (i % 2):6 + 2 * (i % 2), 0:SBC], 0.0, None,
                                ALU.min).then_inc(sb_min, 1)

            def sb_mask(i):
                dve.wait_ge(sb_w, i + 1)
                a, b = diag(wsb[i % 2])
                step(V.tensor_tensor(a, a, keep, ALU.mult))
                V.tensor_tensor(b, b, keep, ALU.mult).then_inc(sb_wm, 1)

            def sb_take(i):
                dve.wait_ge(sb_o, i + 1)
                V.tensor_copy(sbT[:, i, :], ps[:, 4 + 2 * (i % 2), 0:T]).then_inc(sb_out, 1)

            dve.wait_ge(cb_done, 1)
            dve.wait_ge(yoff_done, 1)
            sb_softplus(0)
            sb_softplus(1)
            sb_clip(0)
            sb_clip(1)
            sb_mask(0)
            sb_mask(1)
            sb_take(0)
            sb_take(1)
            sb_softplus(2)
            sb_softplus(3)
            sb_clip(2)
            sb_clip(3)
            sb_mask(2)
            sb_mask(3)
            sb_take(2)
            sb_take(3)
            dve.wait_ge(silu_z, 1)
            V.tensor_tensor(xs[:], xs[:], z, ALU.mult).then_inc(y_full, 1)
            dve.wait_ge(rstd, 2)
            normalise(1, memx, memx, 2)
            take_transposed(1, memT, ROW_MEM)
            dve.wait_ge(rstd, 3)
            for b in range(TB):
                step(V.tensor_scalar(xs[:, b, 0:512], xs[:, b, 0:512], ss[:, 4 + 2 * b:5 + 2 * b], None, ALU.mult))
                V.tensor_scalar(xs[:, b, 512:], xs[:, b, 512:], ss[:, 5 + 2 * b:6 + 2 * b], None,
                                ALU.mult).then_inc(normed, 1)
            take_transposed(2, nT, ROW_SSD)
            dve.wait_ge(gate_sig, 2)
            for n in range(2):
                c = slice(n * SW, (n + 1) * SW)
                s = FIRST["ssd_out"] + 2 * n
                dve.wait_ge(chunk_used, products_done(s))
                V.tensor_tensor(merged[:, :, c], ps[:, 2 * (s % 2):2 * (s % 2) + 2, :], gates[:, :, c],
                                ALU.mult).then_inc(stripe_out["dve"], 1)
                s += 1
                dve.wait_ge(chunk_used, products_done(s))
                V.tensor_tensor(scr2[:], ps[:, 2 * (s % 2):2 * (s % 2) + 2, :],
                                gates[:, :, D + n * SW:D + (n + 1) * SW], ALU.mult).then_inc(stripe_out["dve"], 1)
                dve.wait_ge(stripe_out["dve"], 2 * n + 2)
                i = V.tensor_tensor(merged[:, :, c], merged[:, :, c], scr2[:], ALU.add)
                i.then_inc(normed, 1)
                dve.wait_ge(normed, 3 * TB + n + 1)
            take_transposed(3, nT, None)

            def add_stripes(name):
                for n in range(2):
                    s = FIRST[name] + n
                    hc = h[:, :, n * SW:(n + 1) * SW]
                    dve.wait_ge(chunk_used, products_done(s))
                    V.tensor_tensor(hc, ps[:, 2 * (s % 2):2 * (s % 2) + 2, :], hc,
                                    ALU.add).then_inc(stripe_out["dve"], 1)
                dve.wait_ge(stripe_out["dve"], emptied(FIRST[name] + 1)[1])

            add_stripes("out")
            dve.wait_ge(rstd, 4)
            normalise(4, hn1, h, 8)
            take_transposed(4, nT, ROW_XATTN)
            for hd in range(H_XA):
                dve.wait_ge(xa_lg, hd + 1)
                V.tensor_reduce(xas[:, 0, 2 * hd:2 * hd + 2], ps[:, 4 + hd, :].rearrange("p (b m) -> p b m", b=TB),
                                AX.X, ALU.max, negate=True).then_inc(xa_max, 1)
            for hd in range(H_XA):
                dve.wait_ge(xa_exp, 2 * hd + 2)
                u = slice(2 * hd, 2 * hd + 2)
                step(V.reciprocal(xas[:, 2, u], xas[:, 1, u]))
                V.tensor_tensor(prob[:, u, :], prob[:, u, :], xas[:, 2, u].unsqueeze(2).broadcast_to([P, TB, T]),
                                ALU.mult).then_inc(xa_prob, 1)
            add_stripes("xo")
            dve.wait_ge(rstd, 5)
            normalise(5, hn2, h, 10)
            take_transposed(5, nT, ROW_MOE)
            dve.wait_ge(rt_done, 1)
            step(V.tensor_tensor(lg[:], ps[:, 4, 0:TB * NE].rearrange("p (b e) -> p b e", b=TB),
                                 brt[:].unsqueeze(1).broadcast_to([P, TB, NE]), ALU.add))
            for b in range(TB):
                step(V.max(out=top8[:, b, :], in_=lg[:, b, :]))
                step(V.max_index(out=idx8[:, b, :], in_max=top8[:, b, :], in_values=lg[:, b, :]))
            V.tensor_scalar(rsm[:, 0:TB], top8[:, :, 0], -1.0, None, ALU.mult).then_inc(rt_max, 1)
            step(V.tensor_copy(idxf[:], idx8[:, :, 0:TOPK]))
            dve.wait_ge(consts, N_CONST)
            dve.wait_ge(tr_done, 8)
            step(V.tensor_tensor(oh4, iota_e[:].unsqueeze(1).unsqueeze(1).broadcast_to([P, TB, TOPK, NE]),
                                 idxf[:].unsqueeze(3).broadcast_to([P, TB, TOPK, NE]), ALU.is_equal))
            V.tensor_reduce(mask[:], oh4.rearrange("p b j e -> p b e j"), AX.X, ALU.add).then_inc(rt_mask, 1)
            dve.wait_ge(rt_exp, 2)
            step(V.reciprocal(rsm[:, 4:4 + TB], rsm[:, 2:2 + TB]))
            step(V.tensor_tensor(g4[:], g4[:], rsm[:, 4:4 + TB].unsqueeze(2).broadcast_to([P, TB, TOPK]), ALU.mult))
            step(V.tensor_tensor(ohg, oh4, g4[:].unsqueeze(3).broadcast_to([P, TB, TOPK, NE]), ALU.mult))
            V.tensor_reduce(gate_d[:], ohg.rearrange("p b j e -> p b e j"), AX.X, ALU.add).then_inc(rt_mask, 1)
            dve.wait_ge(rt_mask, 2)
            dve.wait_ge(rk_done, 1)
            step(V.memset(rankx[:, :, NPASS * NE:], -1.0))
            step(V.memset(gatex[:, :, NPASS * NE:], 0.0))
            r0 = rankx[:, :, 0:NE]
            step(V.scalar_tensor_tensor(out=r0, in0=ps[:, 5, 0:TB * NE].rearrange("p (b e) -> p b e", b=TB),
                                        scalar=1.0, in1=mask[:], op0=ALU.add, op1=ALU.mult))
            step(V.tensor_scalar(r0, r0, -1.0, None, ALU.add))
            for p_ in range(NPASS):
                c = slice(p_ * NE, (p_ + 1) * NE)
                if p_:
                    step(V.tensor_scalar(rankx[:, :, c], r0, -float(SLOTS * p_), None, ALU.add))
                step(V.tensor_copy(gatex[:, :, c], gate_d[:]))
            V.tensor_reduce(cnt_f[:], ps[:, 5, 2 * NE:3 * NE], AX.X, ALU.max).then_inc(rk_ready, 1)
            dve.wait_ge(rk_ready, 1)
            V.tensor_copy(cnt_i[:], cnt_f[:]).then_inc(rk_ready, 1)
            step(V.memset(hotT, 0.0))
            V.memset(yb, 0.0).then_inc(yb_ready, 1)

            iota_b = iota_s[:].unsqueeze(1).broadcast_to([P, GE, SLOTS])

            def next_onehot(col, ins_sem):
                for b in range(TB):
                    i = V.tensor_tensor(onehot[:, b], iota_b,
                                        rankx[:, b, bass.ds(col, GE)].unsqueeze(2).broadcast_to([P, GE, SLOTS]),
                                        ALU.is_equal)
                    if b == TB - 1:
                        i.then_inc(ins_sem, 1)

            def take_gathered(buf, k0):
                g = pcol[:, ROW_MOE + k0:ROW_MOE + k0 + 2].unsqueeze(2).broadcast_to([P, 2, T])
                V.tensor_tensor(buf[:, k0:k0 + 2, :], ps[:, 7, :].rearrange("p (k s) -> p k s", k=2), g,
                                ALU.mult).then_inc(gather_out, 1)

            next_onehot(0, hot_ready)
            for k0 in range(0, KD, 2):
                dve.wait_ge(gathered, k0 // 2 + 1)
                take_gathered(xgT[0], k0)

            def experts(it):
                for j in range(BODY):
                    n = it * BODY + j
                    if j % GE == 0:
                        gr = it * 2 + j // GE
                        dve.wait_ge(hot_ready, it * 2 + (j // GE + 1))
                        for b in range(TB):
                            i = V.tensor_tensor(gatehot[:, b],
                                            onehot[:, b].unsqueeze(2).broadcast_to([P, GE, 2, SLOTS]),
                                            gatex[:, b, bass.ds(gr * GE, GE)].unsqueeze(2).unsqueeze(2)
                                            .broadcast_to([P, GE, 2, SLOTS]), ALU.mult)
                        i.then_inc(gatehot_made, 1)
                        dve.wait_ge(chunk_used, it * (BODY * EXP_CH) + (FRONT_CH + (j - 1) * EXP_CH + KD))
                        V.tensor_copy(sel, identx[:, bass.ds(gr * GE, GE)].unsqueeze(2).broadcast_to([NE, GE, SLOTS]))
                        dve.wait_ge(gathered, it * 8 + (j + 4))
                        dve.wait_ge(gatehot_made, it * 2 + (j // GE + 1))
                        next_onehot(gr * GE + GE, hot_ready)
                    dve.wait_ge(chunk_used, it * (BODY * EXP_CH) + (FRONT_CH + j * EXP_CH + KD))
                    V.tensor_scalar(gl, ps[:, 4, :], LIM, None, ALU.min).then_inc(gl_ready, 1)
                    V.tensor_scalar(ul, ps[:, 5, :], LIM, -LIM, ALU.min, ALU.max).then_inc(gu_read, 1)
                    dve.wait_ge(gl_ready, n + 1)
                    dve.wait_ge(gu_read, n + 1)
                    V.scalar_tensor_tensor(out=ul, in0=ul, scalar=1.0, in1=gl, op0=ALU.add,
                                           op1=ALU.mult).then_inc(up_ready, 1)
                    dve.wait_ge(up_ready, n + 1)
                    dve.wait_ge(sg_ready, n + 1)
                    V.tensor_tensor(actv, ul, sg, ALU.mult).then_inc(act_ready, 1)
                    dve.wait_ge(gathered, it * 8 + (j + 5))
                    take_gathered(xgT[1 - j // GE], 2 * (j % GE))
                    dve.wait_ge(chunk_used, it * (BODY * EXP_CH) + (FRONT_CH + (j + 1) * EXP_CH))
                    dve.wait_ge(comb_done, n + 1)
                    V.tensor_copy(yb, ps[:, 6, :]).then_inc(yb_ready, 1)

            with dve.Fori(0, NIT) as g:
                experts(g)
            dve.wait_ge(yb_ready, NE + 1)
            with dve.If(overflow_cond(dve)):
                with dve.Fori(1, NPASS) as p_:
                    with dve.Fori(0, NIT) as g:
                        experts(p_ * NIT + g)
                dve.wait_ge(yb_ready, NPASS * NE + 1)
            V.tensor_copy(cnt_f[:], cnt_i[:]).then_inc(yb_last, 1)
            dve.wait_ge(y_done, 1)
            hf = h[:].rearrange("p b d -> p (b d)")
            V.tensor_tensor(hf, ps[:, 0:4, :].rearrange("p a d -> p (a d)"), hf, ALU.add).then_inc(h_full, 1)
            dve.wait_ge(h_full, 1)
            dve.wait_ge(rstd, 6)
            dve.wait_ge(gf_in, 16)
            for b in range(TB):
                V.scalar_tensor_tensor(out=xn[:, b, :], in0=h[:, b, :], scalar=ss[:, 12 + b:13 + b], in1=gfin,
                                       op0=ALU.mult, op1=ALU.mult).then_inc(out_ready, 1)


_INS = ["x", "mem", "g_mix", "w_in", "conv_w", "conv_b", "dt_bias", "a_log", "d_skip", "g_ssd", "w_ssd_out",
        "w_sb_out", "w_out", "g_xattn", "g_mem", "w_xq", "w_xkv", "w_xo", "g_moe", "w_router", "b_router",
        "w_gu", "b_gu", "w_down", "b_down", "g_final"]


def kernel(**inputs):
    import concourse.bacc as bacc
    from concourse.bass_utils import run_bass_kernel_spmd

    nc = bacc.Bacc("TRN2", target_bir_lowering=False, num_devices=1)
    arrays, args = {}, []
    for name in _INS:
        a = np.ascontiguousarray(inputs[name])
        arrays[f"in_{name}"] = a
        args.append(nc.dram_tensor(f"in_{name}", a.shape, mybir.dt.from_np(a.dtype), kind="ExternalInput").ap())
    args.append(nc.dram_tensor("out_h", (1, T, D), F32, kind="ExternalOutput").ap())
    build(nc, *args)
    r = run_bass_kernel_spmd(nc, [arrays], core_ids=[0])
    return r.results[0]["out_h"]
```

```python
from contextlib import ExitStack

import numpy as np
import concourse.bass as bass
from concourse import mybir

F32 = mybir.dt.float32
F32R = mybir.dt.float32r
BF16 = mybir.dt.bfloat16
U32 = mybir.dt.uint32
I32 = mybir.dt.int32
ALU = mybir.AluOpType
ACT = mybir.ActivationFunctionType
AX = mybir.AxisListType

P = 128
D = 1024
T = 256
TB = T // P
KD = D // P
EPS = 1e-6

H_SSD, PD, NST, GRP = 16, 64, 128, 2
CONV = 4
NCB = (D + 2 * GRP * NST) // P
H_SB, DH = 8, 64
SB_IN = H_SB * DH
H_XA, DX = 4, 128
NE, TOPK, FF = 32, 4, 1024
LIM, ALPHA = 7.0, 1.702

COL_Z, COL_XBC = 0, D
COL_DT = COL_XBC + NCB * P
COL_Q = COL_DT + H_SSD
COL_K = COL_Q + SB_IN
COL_V = COL_K + SB_IN
COL_G = COL_V + SB_IN

RING = 12
RING_MOE = 16
CH = 2048
SW = 512

SLOTS = 64
GE = 4
BODY = 8
NIT = NE // BODY
NPASS = T // SLOTS
GROUPS = NPASS * NE // GE
TABW = (GROUPS + 1) * GE
EXP_CH = KD + FF // P // 2


def stripes():
    s = [("xbc", "w_in", COL_XBC + SW * i, KD, "channel", "act") for i in range(3)]
    s += [("q", "w_in", COL_Q, KD, "channel", "act"), ("k", "w_in", COL_K, KD, "channel", "act"),
          ("v", "w_in", COL_V, KD, "token", "act")]
    s += [("z", "w_in", COL_Z + SW * i, KD, "token", "act") for i in range(2)]
    s += [("gate", "w_in", COL_G + SW * i, KD, "token", "act") for i in range(4)]
    for i in range(2):
        s += [("ssd_out", "w_ssd_out", SW * i, KD, "token", "dve"),
              ("sb_out", "w_sb_out", SW * i, SB_IN // P, "token", "dve")]
    s += [("xk", "w_xkv", 0, KD, "channel", "act")]
    s += [("out", "w_out", SW * i, KD, "token", "dve") for i in range(2)]
    s += [("xv", "w_xkv", H_XA * DX, KD, "token", "act")]
    s += [("xq", "w_xq", 0, KD, "channel", "act")]
    s += [("xo", "w_xo", SW * i, H_XA * DX // P, "token", "dve") for i in range(2)]
    return s


STRIPES = stripes()
FIRST = {}
for _n, _s in enumerate(STRIPES):
    FIRST.setdefault(_s[0], _n)
CHUNKS = [(n, c) for n, st in enumerate(STRIPES) for c in range(st[3] // 4)]
CHUNKS.remove((FIRST["xv"], 1))
CHUNKS.insert(CHUNKS.index((FIRST["xq"], 1)) + 1, (FIRST["xv"], 1))
CHUNK_AT = {c: i for i, c in enumerate(CHUNKS)}
FRONT_CH = len(CHUNKS)
EMPTIED = sorted(range(len(STRIPES)), key=lambda n: CHUNK_AT[(n, STRIPES[n][3] // 4 - 1)])


def emptied(n):
    if STRIPES[n][0] == "xbc":
        return "tap", 8 * (n + 1)
    before = EMPTIED[:EMPTIED.index(n) + 1]
    return STRIPES[n][5], sum(STRIPES[i][5] == STRIPES[n][5] and STRIPES[i][0] != "xbc" for i in before)


def products_done(n):
    return CHUNK_AT[(n, STRIPES[n][3] // 4 - 1)] + 1


SPLIT_CH = 2 * FIRST["ssd_out"]
SPLIT = 3
RING_SPLIT = RING - 2 * SPLIT - 1
LAST = FRONT_CH - RING


def slot(m):
    if m <= LAST:
        return m % RING_SPLIT
    if m <= LAST + RING - RING_SPLIT:
        return RING_SPLIT + m - LAST - 1
    if m < FRONT_CH:
        return slot(m - RING)
    order = list(range(RING, RING_MOE)) + [slot(i) for i in range(LAST, FRONT_CH)]
    return order[(m - FRONT_CH) % RING_MOE]


def slot_free(m):
    before = [i for i in range(m) if slot(i) == slot(m)]
    return before[-1] + 1 if before else (SPLIT_CH if slot(m) >= RING_SPLIT else 0)


def filled(m):
    return 16 * sum(slot(i) == slot(m) for i in range(m + 1))


STEP_CH = BODY * EXP_CH
assert STEP_CH % RING_MOE == 0

assert LAST >= SPLIT_CH

TR_X, TR_Y, TR_MEM, TR_MERGED, TR_H1, TR_H2 = range(6)
NORMED = [1, 3, 5, 7, 8, 9]
SQUARED = {"x": 1, "y": 5, "mem": 7, "h1": 8, "h2": 9, "final": 10}


ROW_MIX, ROW_XATTN, ROW_MEM, ROW_MOE, ROW_SSD = 0, KD, 2 * KD, 3 * KD, 4 * KD
ROW_CW = 5 * KD
ROW_CB = ROW_CW + CONV * NCB
ROWS = ROW_CB + NCB


def build(nc, x, mem, g_mix, w_in, conv_w, conv_b, dt_bias, a_log, d_skip, g_ssd, w_ssd_out,
          w_sb_out, w_out, g_xattn, g_mem, w_xq, w_xkv, w_xo, g_moe, w_router, b_router,
          w_gu, b_gu, w_down, b_down, g_final, out):
    mats = {"w_in": w_in[0], "w_xkv": w_xkv[0], "w_ssd_out": w_ssd_out[0], "w_sb_out": w_sb_out[0],
            "w_out": w_out[0], "w_xq": w_xq[0], "w_xo": w_xo[0]}
    ctx = ExitStack()
    with ctx:
        def sb(name, shape, dt=F32):
            return ctx.enter_context(nc.sbuf_tensor(name, shape, dt))

        def sem(name):
            return ctx.enter_context(nc.semaphore(name))

        def aligned():
            return -(-nc.sbuf_base // 32) * 32

        ring_at = aligned()
        ring = sb("ring", [P, RING, CH])
        h = sb("h", [P, TB, D])
        xn = sb("xn", [P, TB, D])
        nT_at = aligned()
        nT = sb("nT", [P, KD, T])
        xT_hi = nc.alloc_sbuf_tensor_at("xT_hi", [P, KD, T], F32R, offset=ring_at + RING_SPLIT * CH * 4)
        xT_lo = nc.alloc_sbuf_tensor_at("xT_lo", [P, KD, T], F32R, offset=nT_at)
        w_hi, w_lo = (nc.alloc_sbuf_tensor_at(f"w_{name}", [P, SPLIT, CH], F32R,
                                              offset=ring_at + (RING_SPLIT + 1 + i * SPLIT) * CH * 4)
                      for i, name in enumerate(("hi", "lo")))
        xbuf = sb("xbuf", [P, 3136])
        xcT = sb("xcT", [P, NCB, T])
        xs = sb("xs", [P, TB, D])
        qT = sb("qT", [P, H_SB // 2, T])
        kv = sb("kv", [P, CH])
        small = sb("small", [P, CH])
        gates = sb("gates", [P, TB, 2 * D])
        scr = sb("scr", [P, 4, 512])
        junk_t = sb("junk", [P, 2 * TB * TABW])
        prow = sb("prow", [ROWS, P])
        pcol = sb("pcol", [P, ROWS])
        ident = sb("ident", [P, P])
        ones = sb("ones", [P, P])
        nones = sb("nones", [P, P])
        u_incl = sb("u_incl", [P, P])
        u_strict = sb("u_strict", [P, P])
        l_strict = sb("l_strict", [P, P])
        nl_incl = sb("nl_incl", [P, P])
        identx = sb("identx", [NE, TABW])
        iota_s = sb("iota_s", [P, SLOTS])
        iota_e = sb("iota_e", [P, NE])
        w_dt = sb("w_dt", [P, KD, H_SSD])
        wr = sb("wr", [P, KD, NE])
        head_rows = sb("head_rows", [P, 3, H_SSD])
        brt = sb("brt", [P, NE])
        ss = sb("ss", [P, 16])
        mhalf = sb("mhalf", [P, 4])
        lg = sb("lg", [P, TB, NE])
        top8 = sb("top8", [P, TB, 8])
        idx8 = sb("idx8", [P, TB, 8], U32)
        idxf = sb("idxf", [P, TB, TOPK])
        g4 = sb("g4", [P, TB, TOPK])
        rsm = sb("rsm", [P, 8])
        xas = sb("xas", [P, 3, 2 * H_XA])
        mask = sb("mask", [P, TB, NE])
        gate_d = sb("gate_d", [P, TB, NE])
        gateT = sb("gateT", [NE, TB, P])
        cnt_f = sb("cnt_f", [P, 1])
        cnt_i = sb("cnt_i", [P, 1], I32)

        kT = kv[:, 0:D].rearrange("p (c t) -> p c t", t=T)
        v = kv[:, D:].rearrange("p (b d) -> p b d", b=TB)
        scr2 = small[:, 0:1024].rearrange("p (a b) -> p a b", a=2)
        cbm = small[:, 1024:1536].rearrange("p (c l) -> p c l", l=P)
        btok = small[:, 1536:1792].rearrange("p (g n) -> p g n", g=GRP)
        dt4 = small[:, 1792:2048].rearrange("p (a b h) -> p a b h", a=8, b=TB)
        junk = junk_t[:].bitcast(BF16)
        xpad = xbuf[:, 0:NCB * (T + 3)].rearrange("p (c t) -> p c t", t=T + 3)
        z = xbuf[:, 0:TB * D].rearrange("p (b d) -> p b d", b=TB)
        xw = xbuf[:, TB * D:TB * D + D]
        merged = z
        xdt = xn
        memx = xn
        xkT = xn[:, 0, :].rearrange("p (c t) -> p c t", t=T)
        xv = xn[:, 1, :].rearrange("p (b d) -> p b d", b=TB)
        dfac = scr[:, 0:2, :]
        efac = scr[:, 2:4, :]
        s0 = scr[:, 0:2, :]
        memT = scr[:].rearrange("p a b -> p (a b)").rearrange("p (k t) -> p k t", t=T)
        gfac = scr2
        SBC = 3 * P
        xcf = xcT[:].rearrange("p c t -> p (c t)")
        sp = [xcf[:, 768 * i:768 * (i + 1)].rearrange("p (a b) -> p a b", a=2) for i in range(2)]
        wsb = [xcf[:, 768 * (2 + i):768 * (3 + i)].rearrange("p (a b) -> p a b", a=2) for i in range(2)]
        sbT = qT
        xqT = kT
        oT = scr[:, 0:2, :].rearrange("p a b -> p (a b)").rearrange("p (c t) -> p c t", t=T)
        hn1 = z
        hn2 = gates[:, 0, :].rearrange("p (b d) -> p b d", b=TB)
        prob = xs[:].rearrange("p b d -> p (b d)").rearrange("p (u m) -> p u m", m=T)
        probT = gates[:, 1, :].rearrange("p (h m t) -> p h m t", h=H_XA, m=TB)
        rankx, gatex = (junk_t[:, i * TB * TABW:(i + 1) * TB * TABW].rearrange("p (b e) -> p b e", b=TB)
                        for i in range(2))
        bgu = xcf[0:NE, 0:2 * FF]
        bdn = xcf[0:NE, 2 * FF:3 * FF]
        gfin = qT[:].rearrange("p a b -> p (a b)")
        xgT = [xs[:].rearrange("p b d -> p (b d)").rearrange("p (k s) -> p k s", k=KD),
               nT]
        gl = xbuf[:, 0:512]
        ul = xbuf[:, 512:1024]
        sg = xbuf[:, 1024:1536]
        actv = xbuf[:, 1536:2048]
        actT = xbuf[:, 2048:2560].rearrange("p (c s) -> p c s", c=4)
        yb = xbuf[:, 2560:3072]
        onehot = scr[:, 0, :].rearrange("p (b e s) -> p b e s", b=TB, e=GE)
        gatehot = scr[:, 1:3, :].rearrange("p b (e u s) -> p b e u s", e=GE, u=2)
        oh4 = scr[:, 2, 0:TB * TOPK * NE].rearrange("p (b j e) -> p b j e", b=TB, j=TOPK)
        ohg = scr[:, 3, 0:TB * TOPK * NE].rearrange("p (b j e) -> p b j e", b=TB, j=TOPK)
        hotT = scr[:, 3, 2 * P:4 * P].rearrange("p (b t) -> p b t", b=TB)
        sel = scr[0:NE, 3, 0:GE * SLOTS].rearrange("p (e s) -> p e s", e=GE)

        more_slots = [small[:], xn[:].rearrange("p b d -> p (b d)"), gates[:, 1, :], kv[:]]

        def ring_slot(m):
            return ring[:, slot(m), :] if slot(m) < RING else more_slots[slot(m) - RING]

        ps = ctx.enter_context(nc.psum_tensor("ps", [P, 8, 512], F32))

        x_in, prm_in, dtw_in, mem_in, late_in, moe_in, gf_in = map(
            sem, ("x_in", "prm_in", "dtw_in", "mem_in", "late_in", "moe_in", "gf_in"))
        slot_full = [sem(f"slot_full{i}") for i in range(RING_MOE)]
        chunk_used = sem("chunk_used")
        consts = sem("consts")
        sq_done = sem("sq_done")
        rstd, mean_sq = sem("rstd"), sem("mean_sq")
        hi_ready, xhi_ready, xlo_ready = sem("hi_ready"), sem("xhi_ready"), sem("xlo_ready")
        lo_ready = {"dve": sem("lo_ready_dve"), "pool": sem("lo_ready_pool")}
        normed, normed_act, sq_dve = sem("normed"), sem("normed_act"), sem("sq_dve")
        tr_done, tr_out = sem("tr_done"), sem("tr_out")
        pt_done, pcol_ready = sem("pt_done"), sem("pcol_ready")
        pad_zero = sem("pad_zero")
        tap_out, conv_done, silu_done = sem("tap_out"), sem("conv_done"), sem("silu_done")
        stripe_out = {"act": sem("stripe_out_act"), "dve": sem("stripe_out_dve"), "tap": tap_out}
        dt_proj, dt_raw, dt_exp, dt_log, a_ready, da_ready = map(
            sem, ("dt_proj", "dt_raw", "dt_exp", "dt_log", "a_ready", "da_ready"))
        cs_done, cs_exp, cb_done, cbm_ready = map(sem, ("cs_done", "cs_exp", "cb_done", "cbm_ready"))
        xs_tr, xs_out, xdt_ready = sem("xs_tr"), sem("xs_out"), sem("xdt_ready")
        d_ready, seg_done, e_ready, g_ready, ydiag = map(
            sem, ("d_ready", "seg_done", "e_ready", "g_ready", "ydiag"))
        y_taken = sem("y_taken")
        xw_ready, st_done, st_out, yoff_done, yoff_taken = map(
            sem, ("xw_ready", "st_done", "st_out", "yoff_done", "yoff_taken"))
        silu_z, gate_sig, y_full = sem("silu_z"), sem("gate_sig"), sem("y_full")
        sb_lg, sb_exp, sb_log, sb_sp, sb_acc, sb_min, sb_w, sb_wm, sb_o, sb_out = map(
            sem, ("sb_lg", "sb_exp", "sb_log", "sb_sp", "sb_acc", "sb_min", "sb_w", "sb_wm", "sb_o", "sb_out"))
        xa_lg, xa_max, xa_exp, xa_prob, xa_tr, xa_trout, xa_o, xa_oout = map(
            sem, ("xa_lg", "xa_max", "xa_exp", "xa_prob", "xa_tr", "xa_trout", "xa_o", "xa_oout"))
        rt_done, rt_max, rt_exp, rt_mask, rk_done, rk_ready, gt_out = map(
            sem, ("rt_done", "rt_max", "rt_exp", "rt_mask", "rk_done", "rk_ready", "gt_out"))
        hot_ready, gathered, gather_out = sem("hot_ready"), sem("gathered"), sem("gather_out")
        gl_ready, gu_read, sg_ready, act_ready = map(
            sem, ("gl_ready", "gu_read", "sg_ready", "act_ready"))
        ht_done, ht_out, at_done, at_out, yb_ready, comb_done, y_done, yb_last, up_ready, h_full, \
            gatehot_made = map(
            sem, ("ht_done", "ht_out", "at_done", "at_out", "yb_ready", "comb_done", "y_done",
                  "yb_last", "up_ready", "h_full", "gatehot_made"))
        dve_step, act_step = sem("dve_step"), sem("act_step")
        out_sem, out_ready = sem("out_sem"), sem("out_ready")

        block = ctx.enter_context(nc.Block())

        LO_DVE = 2

        def low_part(eng, ops, name, m):
            eng.wait_ge(slot_full[slot(m)], filled(m))
            eng.wait_ge(hi_ready, m + 1)
            ops.tensor_tensor(w_lo[:, m % SPLIT, :], ring_slot(m), w_hi[:, m % SPLIT, :],
                              ALU.subtract).then_inc(lo_ready[name], 1)

        def overflow_cond(eng):
            eng.wait_ge(rk_ready, 2)
            return eng.value_load(cnt_i[0:1, 0:1], min_val=0, max_val=T) > SLOTS

        @block.sync
        def _(sp_):
            sp_.dma_start(h[:], x[0].rearrange("(b p) d -> p b d", p=P)).then_inc(x_in, 16)
            for row, vec, n in ((ROW_MIX, g_mix, KD), (ROW_XATTN, g_xattn, KD), (ROW_MEM, g_mem, KD),
                                (ROW_MOE, g_moe, KD), (ROW_SSD, g_ssd, KD), (ROW_CB, conv_b, NCB)):
                sp_.dma_start(prow[row:row + n, :], vec[0].rearrange("(k p) -> k p", p=P)).then_inc(prm_in, 16)
            sp_.dma_start(prow[ROW_CW:ROW_CB, :],
                          conv_w[0].rearrange("j (k p) -> (j k) p", p=P)).then_inc(prm_in, 16)
            for m, (n, c) in enumerate(CHUNKS):
                _, mat, col, _, _, _ = STRIPES[n]
                if slot_free(m):
                    sp_.wait_ge(chunk_used, slot_free(m))
                src = mats[mat][c * 4 * P:(c + 1) * 4 * P, col:col + SW]
                sp_.dma_start(ring_slot(m).rearrange("p (k n) -> p k n", k=4),
                              src.rearrange("(k p) n -> p k n", p=P)).then_inc(slot_full[slot(m)], 16)
            sp_.wait_ge(xa_o, 2)

            def expert_chunks(it, g):
                for j in range(BODY):
                    for c in range(EXP_CH):
                        m = FRONT_CH + j * EXP_CH + c
                        sp_.wait_ge(chunk_used, it * STEP_CH + (m - RING_MOE + 1))
                        if c < KD:
                            src = w_gu[0, bass.ds(g * BODY + j, 1), c * P:(c + 1) * P, :]
                            sp_.dma_start(ring_slot(m),
                                          src.rearrange("e p n -> (e p) n")).then_inc(slot_full[slot(m)], 16)
                        else:
                            r = (c - KD) * 2 * P
                            src = w_down[0, bass.ds(g * BODY + j, 1), r:r + 2 * P, :]
                            sp_.dma_start(ring_slot(m).rearrange("p (k n) -> p k n", k=2),
                                          src.rearrange("e (k p) n -> p (e k) n", p=P)
                                          ).then_inc(slot_full[slot(m)], 16)

            with sp_.Fori(0, NIT) as g:
                expert_chunks(g, g)
            with sp_.If(overflow_cond(sp_)):
                with sp_.Fori(1, NPASS) as p_:
                    with sp_.Fori(0, NIT) as g:
                        expert_chunks(p_ * NIT + g, g)
            for b in range(TB):
                sp_.wait_ge(out_ready, b + 1)
                sp_.dma_start(out[0, b * P:(b + 1) * P, :], xn[:, b, :]).then_inc(out_sem, 16)
            sp_.wait_ge(out_sem, 16 * TB)

        @block.gpsimd
        def _(pool):
            def root(name, c0, cols, width, dve_sums=0):
                pool.wait_ge(sq_done, SQUARED[name])
                if dve_sums:
                    pool.wait_ge(sq_dve, dve_sums)
                s = ss[:, c0:c0 + cols]
                nc.gpsimd.tensor_scalar(s, s, 1.0 / width, EPS, ALU.mult, ALU.add).then_inc(mean_sq, 1)
                roots[0] += 1
                pool.wait_ge(mean_sq, roots[0])
                nc.gpsimd.tensor_tensor(s, s, mhalf[:, 0:cols], ALU.pow).then_inc(rstd, 1)

            roots = [0]
            nc.gpsimd.memset(ident[:], 0.0).then_inc(consts, 1)
            nc.gpsimd.memset(ones[:], 1.0).then_inc(consts, 1)
            nc.gpsimd.memset(nones[:], -1.0).then_inc(consts, 1)
            nc.gpsimd.memset(mhalf[:], -0.5).then_inc(consts, 1)
            pool.wait_ge(consts, 4)
            nc.gpsimd.affine_select(out=ident[:], in_=ident[:], compare_op=ALU.not_equal, fill=1.0, base=0,
                                    pattern=[[-1, P]], channel_multiplier=1).then_inc(consts, 1)
            root("x", 0, 2, D, 1)
            for dst, src, pat, cm, op in ((u_incl, ones, 1, -1, ALU.is_ge), (u_strict, ones, 1, -1, ALU.is_gt),
                                          (l_strict, ones, -1, 1, ALU.is_gt), (nl_incl, nones, -1, 1, ALU.is_ge)):
                nc.gpsimd.affine_select(out=dst[:], in_=src[:], compare_op=op, fill=0.0, base=0,
                                        pattern=[[pat, P]], channel_multiplier=cm).then_inc(consts, 1)
            nc.gpsimd.iota(iota_s[:], pattern=[[1, SLOTS]], base=0, channel_multiplier=0,
                           allow_small_or_imprecise_dtypes=True).then_inc(consts, 1)
            nc.gpsimd.iota(iota_e[:], pattern=[[1, NE]], base=0, channel_multiplier=0,
                           allow_small_or_imprecise_dtypes=True).then_inc(consts, 1)
            pool.dma_start(w_dt[:], w_in[0, :, COL_DT:COL_Q].rearrange("(k p) n -> p k n", p=P)).then_inc(dtw_in, 16)
            for i, vec in enumerate((dt_bias, a_log, d_skip)):
                pool.dma_start(head_rows[:, i, :], vec[0].partition_broadcast(P)).then_inc(dtw_in, 16)
            pool.wait_ge(consts, 5)
            for c in range(0, TABW, NE):
                w = min(NE, TABW - c)
                nc.gpsimd.tensor_copy(identx[:, c:c + w], ident[0:NE, 0:w]).then_inc(consts, 1)
            pool.dma_start(wr[:], w_router[0].rearrange("(k p) n -> p k n", p=P)).then_inc(late_in, 16)
            pool.dma_start(brt[:], b_router[0].partition_broadcast(P)).then_inc(late_in, 16)
            for m in range(LO_DVE, 19):
                low_part(pool, nc.gpsimd, "pool", m)
            pool.wait_ge(ydiag, 8)
            pool.wait_ge(xw_ready, 1)
            pool.dma_start(memx[:], mem[0].rearrange("(b p) d -> p b d", p=P)).then_inc(mem_in, 16)
            for m in range(19, 23):
                low_part(pool, nc.gpsimd, "pool", m)
            root("y", 4, 4, D // GRP)
            for m in range(23, SPLIT_CH):
                low_part(pool, nc.gpsimd, "pool", m)
            pool.wait_ge(sb_o, 4)
            pool.dma_start(bgu, b_gu[0]).then_inc(moe_in, 16)
            pool.dma_start(bdn, b_down[0]).then_inc(moe_in, 16)
            root("mem", 2, 2, D)
            pool.wait_ge(chunk_used, products_done(FIRST["sb_out"] + 2))
            pool.dma_start(gfin, g_final.partition_broadcast(P)).then_inc(gf_in, 16)
            root("h1", 8, 2, D, 2)
            root("h2", 10, 2, D, 3)
            root("final", 12, 2, D, 4)

        N_CONST = 5 + 4 + 2 + -(-TABW // NE)

        @block.tensor
        def _(pe):
            mm = nc.tensor.matmul

            def chunk(m):
                pe.wait_ge(slot_full[slot(m)], filled(m))
                return ring_slot(m).rearrange("p (k n) -> p k n", k=4)

            def stripe(n, src, parts=(0, 1), tr=None):
                _, _, _, kt, layout, _ = STRIPES[n]
                b0 = 2 * (n % 2)
                if n >= 2 and parts[0] == 0:
                    eng, count = emptied(n - 2)
                    pe.wait_ge(stripe_out[eng], count)
                if tr is not None and parts[0] == 0:
                    pe.wait_ge(tr_out, 4 * tr + 2)
                for c in parts if kt > 4 else (0,):
                    if tr is not None and c:
                        pe.wait_ge(tr_out, 4 * tr + 4)
                    if layout == "channel":
                        channel_products(n, src, c, b0)
                    else:
                        token_products(n, src, c, b0)

            def pairs(m, src):
                if src is not None:
                    return [(chunk(m), src)]
                eng = "dve" if m < LO_DVE else "pool"
                pe.wait_ge(lo_ready[eng], m + 1 - (0 if m < LO_DVE else LO_DVE))
                hi, lo = (w[:, m % SPLIT, :].rearrange("p (k n) -> p k n", k=4) for w in (w_hi, w_lo))
                return [(hi, xT_hi), (lo, xT_hi), (hi, xT_lo)]

            def channel_products(n, src, c, b0):
                passes = pairs(CHUNK_AT[(n, c)], src)
                for cb in range(4):
                    for k in range(4):
                        for q, (w, a) in enumerate(passes):
                            i = mm(ps[:, b0 + cb // 2, (cb % 2) * T:(cb % 2 + 1) * T],
                                   w[:, k, cb * P:(cb + 1) * P], a[:, 4 * c + k, :],
                                   start=(c == 0 and k == 0 and q == 0 and cb % 2 == 0),
                                   stop=(c == 1 and k == 3 and q == len(passes) - 1), skip_group_check=True)
                i.then_inc(chunk_used, 1)

            def token_products(n, src, c, b0):
                passes = pairs(CHUNK_AT[(n, c)], src)
                for b in range(TB):
                    for k in range(4):
                        for q, (w, a) in enumerate(passes):
                            i = mm(ps[:, b0 + b, :], a[:, 4 * c + k, b * P:(b + 1) * P], w[:, k, :],
                                   start=(c == 0 and k == 0 and q == 0),
                                   stop=(4 * c + k == STRIPES[n][3] - 1 and q == len(passes) - 1))
                i.then_inc(chunk_used, 1)

            def transposes(n, src):
                for half in range(2):
                    for b in range(TB):
                        if half == 0 and n in (TR_X, TR_H1, TR_H2) and b == 0:
                            pe.wait_ge(normed_act, (TR_X, TR_H1, TR_H2).index(n) + 1)
                        elif half == 0:
                            pe.wait_ge(normed, NORMED[n])
                        for k in range(4):
                            i = nc.tensor.transpose(ps[:, 4 + 2 * b + half, k * P:(k + 1) * P],
                                                    src[:, b, (4 * half + k) * P:(4 * half + k + 1) * P], ident[:])
                        i.then_inc(tr_done, 1)

            pe.wait_ge(prm_in, 16 * 7)
            pe.wait_ge(consts, 9)
            nc.tensor.transpose(ps[:, 3, 0:ROWS], prow[:], ident[0:ROWS, 0:ROWS]).then_inc(pt_done, 1)
            transposes(TR_X, xn)
            pe.wait_ge(xlo_ready, 2)
            for n in range(3):
                stripe(n, None)
            pe.wait_ge(dtw_in, 64)
            for b in range(TB):
                for k in range(KD):
                    for q, a in enumerate((xT_hi, xT_lo)):
                        i = mm(ps[:, 4, b * H_SSD:(b + 1) * H_SSD], a[:, k, b * P:(b + 1) * P].bitcast(F32),
                               w_dt[:, k, :], start=(k == 0 and q == 0), stop=(k == KD - 1 and q == 1))
            i.then_inc(dt_proj, 1)
            stripe(FIRST["q"], None)
            pe.wait_ge(da_ready, 1)
            da = dt4[:, 5, :, :].rearrange("p b h -> p (b h)")
            mm(ps[:, 4, 32:64], u_incl[:], da, start=True, stop=True)
            mm(ps[:, 4, 64:96], l_strict[:], da, start=True, stop=True).then_inc(cs_done, 1)
            stripe(FIRST["k"], None)
            pe.wait_ge(silu_done, 3)
            for b in range(TB):
                for g in range(GRP):
                    i = mm(ps[:, 5, (b * GRP + g) * P:(b * GRP + g + 1) * P], xcT[:, 8 + g, b * P:(b + 1) * P],
                           xcT[:, 10 + g, b * P:(b + 1) * P], start=True, stop=True)
            i.then_inc(cb_done, 1)

            def xs_transposes(half):
                if half:
                    pe.wait_ge(xs_out, 2)
                for b in range(TB):
                    for k in range(4):
                        i = nc.tensor.transpose(ps[:, 6 + b, k * P:(k + 1) * P],
                                                xcT[:, 4 * half + k, b * P:(b + 1) * P], ident[:])
                i.then_inc(xs_tr, 1)

            xs_transposes(0)
            stripe(FIRST["v"], None)
            xs_transposes(1)
            pe.wait_ge(cs_exp, 1)
            for g in range(GRP):
                i = nc.tensor.transpose(ps[:, 4, g * P:(g + 1) * P], xcT[:, 8 + g, 0:P], ident[:])
            i.then_inc(xs_tr, 1)

            def seg(j):
                pe.wait_ge(d_ready, j + 1)
                if j >= 2:
                    pe.wait_ge(e_ready, j - 1)
                else:
                    pe.wait_ge(xs_out, 4)
                mm(ps[:, 6 + j % 2, :], l_strict[:], dfac[:, j % 2, :], start=True, stop=True).then_inc(seg_done, 1)

            def y_diag(j):
                pe.wait_ge(g_ready, j + 1)
                b, q = j // 4, j % 4
                if j == 0:
                    pe.wait_ge(xdt_ready, 1)
                    pe.wait_ge(xs_out, 5)
                if b == 1 and q % 2 == 0:
                    pe.wait_ge(y_taken, q // 2 + 1)
                for i4 in range(4):
                    hd = 4 * q + i4
                    i = mm(ps[:, 4 + q // 2, (hd % 8) * PD:(hd % 8 + 1) * PD],
                           gfac[:, j % 2, i4 * P:(i4 + 1) * P], xdt[:, b, hd * PD:(hd + 1) * PD],
                           start=True, stop=True)
                i.then_inc(ydiag, 1)

            def states():
                pe.wait_ge(xw_ready, 1)
                pe.wait_ge(e_ready, 8)
                for g in range(GRP):
                    i = mm(ps[:, 6 + g, :], btok[:, g, :], xw[:, g * 512:(g + 1) * 512], start=True, stop=True)
                i.then_inc(st_done, 1)

            def y_off():
                pe.wait_ge(st_out, 1)
                for g in range(GRP):
                    i = mm(ps[:, 6 + g, :], xcT[:, 10 + g, P:2 * P], s0[:, g, :], start=True, stop=True)
                i.then_inc(yoff_done, 1)

            seg(0)
            seg(1)
            for r in range(1, 5):
                stripe(FIRST["z"] + (r - 1) // 2, None, parts=((r - 1) % 2,))
                y_diag(2 * r - 2)
                y_diag(2 * r - 1)
                if r < 4:
                    seg(2 * r)
                    seg(2 * r + 1)
            states()
            stripe(FIRST["gate"], None, parts=(0,))
            y_off()
            stripe(FIRST["gate"], None, parts=(1,))

            def sb_logits(i):
                b0 = 4 + 2 * (i % 2)
                if i == 0:
                    pe.wait_ge(y_taken, 4)
                elif i == 1:
                    pe.wait_ge(yoff_taken, 1)
                else:
                    pe.wait_ge(sb_out, i - 1)
                for e in range(2):
                    r = slice(64 * e, 64 * e + 64)
                    mm(ps[:, b0 + e, 0:T], kT[r, i, 0:P], qT[r, i, :], start=True, stop=False,
                       skip_group_check=True)
                    j = mm(ps[:, b0 + e, T:SBC], kT[r, i, P:T], qT[r, i, P:T], start=False, stop=False,
                           skip_group_check=True)
                j.then_inc(sb_lg, 1)

            def sb_stay(i):
                b0 = 4 + 2 * (i % 2)
                pe.wait_ge(sb_sp, i + 1)
                for e in range(2):
                    s = sp[i % 2][:, e, :]
                    mm(ps[:, b0 + e, 0:T], nl_incl[:], s[:, 0:T], start=False, stop=False, skip_group_check=True)
                    mm(ps[:, b0 + e, T:SBC], nl_incl[:], s[:, T:SBC], start=False, stop=False,
                       skip_group_check=True)
                    j = mm(ps[:, b0 + e, P:T], nones[:], s[:, T:SBC], start=False, stop=True,
                           skip_group_check=True)
                j.then_inc(sb_acc, 1)

            def sb_values(i):
                b0 = 4 + 2 * (i % 2)
                pe.wait_ge(sb_wm, i + 1)
                for e in range(2):
                    hd = 2 * i + e
                    o = ps[64 * e:64 * e + 64, b0, :]
                    mm(o[:, 0:T], v[:, 0, hd * DH:(hd + 1) * DH], wsb[i % 2][:, e, 0:T], start=True, stop=False,
                       skip_group_check=True)
                    j = mm(o[:, P:T], v[:, 1, hd * DH:(hd + 1) * DH], wsb[i % 2][:, e, T:SBC], start=False,
                           stop=True, skip_group_check=True)
                j.then_inc(sb_o, 1)

            sb_logits(0)
            sb_logits(1)
            stripe(FIRST["gate"] + 1, None, parts=(0,))
            sb_stay(0)
            sb_stay(1)
            stripe(FIRST["gate"] + 1, None, parts=(1,))
            sb_values(0)
            sb_values(1)
            stripe(FIRST["gate"] + 2, None, parts=(0,))
            sb_logits(2)
            sb_logits(3)
            stripe(FIRST["gate"] + 2, None, parts=(1,))
            sb_stay(2)
            sb_stay(3)
            stripe(FIRST["gate"] + 3, None, parts=(0,))
            sb_values(2)
            sb_values(3)
            stripe(FIRST["gate"] + 3, None, parts=(1,))
            pe.wait_ge(sb_out, 4)
            transposes(TR_Y, xs)
            for n in range(2):
                stripe(FIRST["ssd_out"] + 2 * n, nT, tr=TR_Y)
                stripe(FIRST["sb_out"] + 2 * n, sbT)
            transposes(TR_MEM, memx)
            stripe(FIRST["xk"], memT, parts=(0,), tr=TR_MEM)
            pe.wait_ge(tr_out, 4 * TR_MEM + 4)
            transposes(TR_MERGED, merged)
            stripe(FIRST["xk"], memT, parts=(1,))
            for n in range(2):
                stripe(FIRST["out"] + n, nT, tr=TR_MERGED)
            stripe(FIRST["xv"], memT, parts=(0,))
            transposes(TR_H1, hn1)
            stripe(FIRST["xq"], nT, tr=TR_H1)
            pe.wait_ge(stripe_out["act"], emptied(FIRST["xq"])[1])
            for hd in range(H_XA):
                for b in range(TB):
                    i = mm(ps[:, 4 + hd, b * T:(b + 1) * T], xqT[:, hd, b * P:(b + 1) * P], xkT[:, hd, :],
                           start=True, stop=True)
                i.then_inc(xa_lg, 1)
            stripe(FIRST["xv"], memT, parts=(1,))
            pe.wait_ge(stripe_out["act"], emptied(FIRST["xv"])[1])
            for hd in range(H_XA):
                pe.wait_ge(xa_prob, hd + 1)
                for mb in range(TB):
                    for b in range(TB):
                        i = nc.tensor.transpose(ps[:, 4 + hd, mb * T + b * P:mb * T + (b + 1) * P],
                                                prob[:, 2 * hd + b, mb * P:(mb + 1) * P], ident[:])
                i.then_inc(xa_tr, 1)
            for hd in range(H_XA):
                pe.wait_ge(xa_trout, hd + 1)
                if hd == 0:
                    pe.wait_ge(xa_trout, 2)
                for mb in range(TB):
                    i = mm(ps[:, 4 + hd // 2, (hd % 2) * T:(hd % 2 + 1) * T], xv[:, mb, hd * DX:(hd + 1) * DX],
                           probT[:, hd, mb, :], start=(mb == 0), stop=(mb == TB - 1))
                if hd % 2:
                    i.then_inc(xa_o, 1)
            pe.wait_ge(xa_oout, 2)
            for n in range(2):
                stripe(FIRST["xo"] + n, oT)
            transposes(TR_H2, hn2)
            pe.wait_ge(tr_out, 24)
            pe.wait_ge(late_in, 32)
            for b in range(TB):
                for k in range(KD):
                    i = mm(ps[:, 4, b * NE:(b + 1) * NE], nT[:, k, b * P:(b + 1) * P], wr[:, k, :],
                           start=(k == 0), stop=(k == KD - 1))
            i.then_inc(rt_done, 1)
            pe.wait_ge(rt_mask, 1)
            mm(ps[:, 5, 0:NE], u_strict[:], mask[:, 0, :], start=True, stop=True)
            mm(ps[:, 5, NE:2 * NE], ones[:], mask[:, 0, :], start=True, stop=False)
            mm(ps[:, 5, NE:2 * NE], u_strict[:], mask[:, 1, :], start=False, stop=True)
            mm(ps[:, 5, 2 * NE:3 * NE], ones[:], mask[:, 0, :], start=True, stop=False)
            mm(ps[:, 5, 2 * NE:3 * NE], ones[:], mask[:, 1, :], start=False, stop=True).then_inc(rk_done, 1)
            pe.wait_ge(rt_mask, 2)
            for b in range(TB):
                i = nc.tensor.transpose(ps[0:NE, 4, b * P:(b + 1) * P], gate_d[:, b, :], ident[:])
            i.then_inc(rk_done, 1)
            def gather(k0, bank=7):
                for k in range(2):
                    for b in range(TB):
                        i = mm(ps[:, bank, k * T:(k + 1) * T], hn2[:, b, (k0 + k) * P:(k0 + k + 1) * P],
                               onehot[:, b, :, :].rearrange("p e s -> p (e s)"), start=(b == 0), stop=(b == 1))
                i.then_inc(gathered, 1)

            pe.wait_ge(hot_ready, 1)
            for k0 in range(0, KD, 2):
                if k0 >= 4:
                    pe.wait_ge(gather_out, k0 // 2 - 1)
                gather(k0, 7 - k0 // 2 % 2)

            pe.wait_ge(gt_out, 1)
            pe.wait_ge(moe_in, 32)
            pe.wait_ge(stripe_out["dve"], emptied(FIRST["xo"] + 1)[1])
            for b in range(TB):
                for half in range(2):
                    mm(ps[:, 2 * b + half, :], gateT[:, b, :], bdn[:, half * 512:(half + 1) * 512],
                       start=True, stop=False, skip_group_check=True)

            def combine(done=comb_done, each=False):
                for b in range(TB):
                    if b and each:
                        i.then_inc(done, 1)
                    for half in range(2):
                        r = slice(64 * half, 64 * half + 64)
                        i = mm(ps[:, 2 * b + half, :], hotT[r, b, :], yb[r, :], start=False, stop=False,
                               skip_group_check=True)
                i.then_inc(done, 1)

            def experts(it):
                for j in range(BODY):
                    n = it * BODY + j
                    xg = xgT[j // GE]
                    if j % GE == 0:
                        pe.wait_ge(hot_ready, it * 2 + (j // GE + 2))
                        pe.wait_ge(gather_out, it * 8 + (4 * (j // GE) + 4))
                    for q in range(2):
                        for half in range(2):
                            mm(ps[64 * half:64 * half + 64, 4 + q, :], sel[:, j % GE, :],
                               bgu[:, q * FF + half * 512:q * FF + half * 512 + 512],
                               start=True, stop=False, skip_group_check=True)
                    for k in range(KD):
                        m = FRONT_CH + j * EXP_CH + k
                        pe.wait_ge(slot_full[slot(m)], it * (16 * STEP_CH // RING_MOE) + filled(m))
                        w = ring_slot(m)
                        for q in range(2):
                            for half in range(2):
                                i = mm(ps[64 * half:64 * half + 64, 4 + q, :],
                                       xg[:, k, (j % GE) * SLOTS:(j % GE + 1) * SLOTS],
                                       w[:, q * FF + half * 512:q * FF + half * 512 + 512],
                                       start=False, stop=(k == KD - 1), skip_group_check=True)
                        i.then_inc(chunk_used, 1)
                    pe.wait_ge(yb_ready, n + 1)
                    combine()
                    gather(2 * (j % GE))
                    for b in range(TB):
                        i = nc.tensor.transpose(ps[:, 6, b * P:(b + 1) * P],
                                                gatehot[:, b, j % GE].rearrange("p u s -> p (u s)"),
                                                ident[:])
                    i.then_inc(ht_done, 1)
                    pe.wait_ge(gather_out, it * 8 + (j + 5))
                    pe.wait_ge(act_ready, n + 1)
                    for c in range(4):
                        i = nc.tensor.transpose(ps[:, 7, c * P:(c + 1) * P], actv[:, c * P:(c + 1) * P], ident[:])
                    i.then_inc(at_done, 1)
                    pe.wait_ge(ht_out, n + 1)
                    pe.wait_ge(at_out, n + 1)
                    for k in range(FF // P):
                        m = FRONT_CH + j * EXP_CH + KD + k // 2
                        if k % 2 == 0:
                            pe.wait_ge(slot_full[slot(m)], it * (16 * STEP_CH // RING_MOE) + filled(m))
                        w = ring_slot(m).rearrange("p (k n) -> p k n", k=2)
                        fh, c = k // 4, k % 4
                        for half in range(2):
                            i = mm(ps[64 * half:64 * half + 64, 6, :], actT[:, c, fh * 64:fh * 64 + 64],
                                   w[:, k % 2, half * 512:(half + 1) * 512],
                                   start=(k == 0), stop=(k == FF // P - 1), skip_group_check=True)
                        if k % 2:
                            i.then_inc(chunk_used, 1)

            with pe.Fori(0, NIT) as g:
                experts(g)
            with pe.If(overflow_cond(pe)):
                with pe.Fori(1, NPASS) as p_:
                    with pe.Fori(0, NIT) as g:
                        experts(p_ * NIT + g)
            pe.wait_ge(yb_last, 1)
            combine(y_done, each=True)

        @block.scalar
        def _(act):
            af = nc.scalar.activation
            count = [0]

            def step(ins):
                count[0] += 1
                ins.then_inc(act_step, 1)
                act.wait_ge(act_step, count[0])

            sq = [0]

            def squares(src, c0):
                if sq[0]:
                    act.wait_ge(sq_done, sq[0])
                sq[0] += 1
                af(junk[:, 0:src.shape[1]], src, ACT.Square, accum_out=ss[:, c0:c0 + 1]).then_inc(sq_done, 1)

            split = [0]

            def splits_to(last):
                for m in range(split[0], min(last + 1, SPLIT_CH)):
                    if m >= SPLIT:
                        act.wait_ge(chunk_used, m - SPLIT + 1)
                    act.wait_ge(slot_full[slot(m)], filled(m))
                    af(w_hi[:, m % SPLIT, :], ring_slot(m), ACT.Copy).then_inc(hi_ready, 1)
                    split[0] = m + 1

            def normalise(dst, src, c0, rstds):
                act.wait_ge(rstd, rstds)
                af(dst[:, 0, :], src[:, 0, :], ACT.Copy, scale=ss[:, c0:c0 + 1]).then_inc(normed_act, 1)

            def empty(n, func=ACT.Copy, scale=1.0, ahead=True):
                name, _, _, _, layout, _ = STRIPES[n]
                b0, i = 2 * (n % 2), n - FIRST[name]
                splits_to(products_done(n) + SPLIT - 2)
                act.wait_ge(chunk_used, products_done(n))
                if ahead:
                    splits_to(products_done(n) + SPLIT - 1)
                src = ps[:, b0:b0 + 2, :]
                if layout == "channel":
                    src = src.rearrange("p b (c t) -> p (b c) t", t=T)
                    dst = {"q": qT, "k": kT, "xk": xkT, "xq": xqT}[name][:, 0:4, :]
                else:
                    dst = {"v": lambda: v[:, :, :], "xv": lambda: xv,
                           "z": lambda: z[:, :, i * SW:(i + 1) * SW],
                           "gate": lambda: gates[:, :, i * SW:(i + 1) * SW]}[name]()
                return af(dst, src, func, scale=scale).then_inc(stripe_out["act"], 1)

            act.wait_ge(consts, 5)
            act.wait_ge(x_in, 16)
            squares(h[:, 0, :], 0)
            normalise(xn, h, 0, 1)
            splits_to(0)
            for half in range(2):
                act.wait_ge(tr_out, 2 * half + 2)
                af(xT_hi[:, 4 * half:4 * half + 4, :], nT[:, 4 * half:4 * half + 4, :],
                   ACT.Copy).then_inc(xhi_ready, 1)
            splits_to(2)
            act.wait_ge(pad_zero, 1)
            act.wait_ge(pcol_ready, 1)
            for n in range(3):
                splits_to(products_done(n) + SPLIT - 2)
                act.wait_ge(chunk_used, products_done(n))
                splits_to(products_done(n) + SPLIT - 1)
                for cb in range(4):
                    c = 4 * n + cb
                    src = ps[:, 2 * (n % 2) + cb // 2, (cb % 2) * T:(cb % 2 + 1) * T]
                    af(xpad[:, c, 3:], src, ACT.Copy).then_inc(tap_out, 1)
                    af(xcT[:, c, :], src, ACT.Identity, bias=pcol[:, ROW_CB + c:ROW_CB + c + 1],
                       scale=pcol[:, ROW_CW + 3 * NCB + c:ROW_CW + 3 * NCB + c + 1]).then_inc(tap_out, 1)
            act.wait_ge(dtw_in, 64)
            act.wait_ge(dt_raw, 2)
            af(dt4[:, 2], dt4[:, 1], ACT.Exp, scale=-1.0).then_inc(dt_exp, 1)
            act.wait_ge(dt_exp, 1)
            af(dt4[:, 3], dt4[:, 2], ACT.Ln, bias=1.0).then_inc(dt_log, 1)
            af(head_rows[:, 1, :], head_rows[:, 1, :], ACT.Exp).then_inc(a_ready, 1)
            for n in range(3):
                act.wait_ge(conv_done, 4 * n + 4)
                af(xcT[:, 4 * n:4 * n + 4, :], xcT[:, 4 * n:4 * n + 4, :], ACT.Silu).then_inc(silu_done, 1)
                if n == 1:
                    splits_to(9)
            empty(FIRST["q"], scale=DH ** -0.5)
            act.wait_ge(cs_done, 1)
            af(dt4[:, 6:8].rearrange("p a b h -> p (a b h)"), ps[:, 4, 32:96], ACT.Exp).then_inc(cs_exp, 1)
            empty(FIRST["k"])

            def xs_copy(half):
                act.wait_ge(xs_tr, half + 1)
                for b in range(TB):
                    af(xs[:, b, half * 512:(half + 1) * 512], ps[:, 6 + b, :], ACT.Copy).then_inc(xs_out, 1)

            xs_copy(0)
            empty(FIRST["v"], ahead=False)
            xs_copy(1)
            act.wait_ge(xs_tr, 3)
            af(btok[:].rearrange("p g n -> p (g n)"), ps[:, 4, 0:GRP * NST], ACT.Copy).then_inc(xs_out, 1)

            def seg_exp(j):
                act.wait_ge(seg_done, j + 1)
                if j >= 2:
                    act.wait_ge(g_ready, j - 1)
                af(efac[:, j % 2, :], ps[:, 6 + j % 2, :], ACT.Exp).then_inc(e_ready, 1)

            for j in range(4):
                seg_exp(j)
                if j == 1:
                    splits_to(14)
            empty(FIRST["z"])
            for j in range(4, 8):
                seg_exp(j)
                if j == 5:
                    splits_to(16)
            empty(FIRST["z"] + 1)
            act.wait_ge(st_done, 1)
            act.wait_ge(seg_done, 8)
            af(s0, ps[:, 6:8, :], ACT.Copy).then_inc(st_out, 1)
            splits_to(19)
            empty(FIRST["gate"])

            def sb_softplus(pair):
                for i in pair:
                    act.wait_ge(sb_lg, i + 1)
                    if i == 0:
                        act.wait_ge(cb_done, 1)
                        act.wait_ge(yoff_done, 1)
                    if i >= 2:
                        act.wait_ge(sb_acc, i - 1)
                    af(sp[i % 2], ps[:, 4 + 2 * (i % 2):6 + 2 * (i % 2), 0:SBC], ACT.Abs).then_inc(act_step, 1)
                count[0] += 2
                act.wait_ge(act_step, count[0])
                for i in pair:
                    af(sp[i % 2], sp[i % 2], ACT.Exp, scale=-1.0).then_inc(act_step, 1)
                count[0] += 2
                act.wait_ge(act_step, count[0])
                for i in pair:
                    af(sp[i % 2], sp[i % 2], ACT.Ln, bias=1.0).then_inc(sb_log, 1)

            def sb_weights(i):
                act.wait_ge(sb_min, i + 1)
                af(wsb[i % 2], wsb[i % 2], ACT.Exp).then_inc(sb_w, 1)

            sb_softplus((0, 1))
            splits_to(21)
            act.wait_ge(stripe_out["act"], emptied(FIRST["z"] + 1)[1])
            af(z, z, ACT.Silu).then_inc(silu_z, 1)
            sb_weights(0)
            sb_weights(1)
            empty(FIRST["gate"] + 1)
            act.wait_ge(y_full, 1)
            for b in range(TB):
                for g in range(GRP):
                    squares(xs[:, b, g * 512:(g + 1) * 512], 4 + 2 * b + g)
            splits_to(23)
            sb_softplus((2, 3))
            empty(FIRST["gate"] + 2)
            sb_weights(2)
            sb_weights(3)
            act.wait_ge(mem_in, 16)
            for b in range(TB):
                squares(memx[:, b, :], 2 + b)
            empty(FIRST["gate"] + 3)
            act.wait_ge(stripe_out["act"], emptied(FIRST["gate"] + 3)[1])
            for half in range(2):
                af(gates[:, half, :], gates[:, half, :], ACT.Sigmoid).then_inc(gate_sig, 1)
            empty(FIRST["xk"])
            act.wait_ge(stripe_out["dve"], emptied(FIRST["out"] + 1)[1])
            squares(h[:, 0, :], 8)
            normalise(hn1, h, 8, 4)
            empty(FIRST["xq"], scale=DX ** -0.5)
            for hd in range(H_XA):
                act.wait_ge(xa_max, hd + 1)
                for b in range(TB):
                    u = 2 * hd + b
                    af(prob[:, u, :], ps[:, 4 + hd, b * T:(b + 1) * T], ACT.Exp, bias=xas[:, 0, u:u + 1],
                       accum_out=xas[:, 1, u:u + 1]).then_inc(xa_exp, 1)
            empty(FIRST["xv"])
            for hd in range(H_XA):
                act.wait_ge(xa_tr, hd + 1)
                af(probT[:, hd].rearrange("p m t -> p (m t)"), ps[:, 4 + hd, :], ACT.Copy).then_inc(xa_trout, 1)
            for i in range(2):
                act.wait_ge(xa_o, i + 1)
                af(oT[:, 2 * i:2 * i + 2, :].rearrange("p h t -> p (h t)"), ps[:, 4 + i, :],
                   ACT.Copy).then_inc(xa_oout, 1)
            act.wait_ge(stripe_out["dve"], emptied(FIRST["xo"] + 1)[1])
            squares(h[:, 0, :], 10)
            normalise(hn2, h, 10, 5)
            act.wait_ge(rt_max, 1)
            for b in range(TB):
                af(g4[:, b, :], top8[:, b, 0:TOPK], ACT.Exp, bias=rsm[:, b:b + 1],
                   accum_out=rsm[:, 2 + b:3 + b]).then_inc(rt_exp, 1)
            act.wait_ge(rk_done, 2)
            af(gateT[:].rearrange("p b t -> p (b t)"), ps[0:NE, 4, 0:T], ACT.Copy).then_inc(gt_out, 1)

            def experts(it):
                for j in range(BODY):
                    n = it * BODY + j
                    act.wait_ge(gl_ready, n + 1)
                    af(sg, gl, ACT.Sigmoid, scale=ALPHA).then_inc(sg_ready, 1)
                    act.wait_ge(ht_done, n + 1)
                    af(hotT.rearrange("p b t -> p (b t)"), ps[:, 6, 0:2 * P], ACT.Copy).then_inc(ht_out, 1)
                    act.wait_ge(at_done, n + 1)
                    af(actT.rearrange("p c s -> p (c s)"), ps[:, 7, :], ACT.Copy).then_inc(at_out, 1)

            with act.Fori(0, NIT) as g:
                experts(g)
            with act.If(overflow_cond(act)):
                with act.Fori(1, NPASS) as p_:
                    with act.Fori(0, NIT) as g:
                        experts(p_ * NIT + g)
            act.wait_ge(h_full, 1)
            squares(h[:, 0, :], 12)

        @block.vector
        def _(dve):
            V = nc.vector
            count = [0]

            def step(ins):
                count[0] += 1
                ins.then_inc(dve_step, 1)
                dve.wait_ge(dve_step, count[0])

            def squares(dst, src, c0):
                V.tensor_tensor_reduce(out=dst[:, 1, :], in0=src[:, 1, :], in1=src[:, 1, :], scale=1.0, scalar=0.0,
                                       op0=ALU.mult, op1=ALU.add,
                                       accum_out=ss[:, c0 + 1:c0 + 2]).then_inc(sq_dve, 1)

            def normalise(dst, src, c0, blocks=(1,)):
                for b in blocks:
                    V.tensor_scalar(dst[:, b, :], src[:, b, :], ss[:, c0 + b:c0 + b + 1], None,
                                    ALU.mult).then_inc(normed, 1)

            def take_transposed(n, dst, row):
                for half in range(2):
                    for b in range(TB):
                        dve.wait_ge(tr_done, 4 * n + 2 * half + b + 1)
                        src = ps[:, 4 + 2 * b + half, :].rearrange("p (k t) -> p k t", k=4)
                        d = dst[:, 4 * half:4 * half + 4, b * P:(b + 1) * P]
                        if row is None:
                            V.tensor_copy(d, src).then_inc(tr_out, 1)
                        else:
                            g = pcol[:, row + 4 * half:row + 4 * half + 4].unsqueeze(2).broadcast_to([P, 4, P])
                            V.tensor_tensor(d, src, g, ALU.mult).then_inc(tr_out, 1)

            V.memset(xpad[:, :, 0:3], 0.0).then_inc(pad_zero, 1)
            dve.wait_ge(x_in, 16)
            squares(xn, h, 0)
            dve.wait_ge(rstd, 1)
            normalise(xn, h, 0)
            dve.wait_ge(pt_done, 1)
            V.tensor_copy(pcol[:], ps[:, 3, 0:ROWS]).then_inc(pcol_ready, 1)
            dve.wait_ge(pcol_ready, 1)
            take_transposed(TR_X, nT, ROW_MIX)
            dve.wait_ge(tr_out, 4)
            for half in range(2):
                dve.wait_ge(xhi_ready, half + 1)
                k = slice(4 * half, 4 * half + 4)
                V.tensor_tensor(xT_lo[:, k, :], nT[:, k, :], xT_hi[:, k, :], ALU.subtract).then_inc(xlo_ready, 1)
            for m in range(LO_DVE):
                low_part(dve, V, "dve", m)

            def convolve(c):
                for tap in range(3):
                    if tap == 0:
                        dve.wait_ge(tap_out, 2 * c + 2)
                    i = V.scalar_tensor_tensor(out=xcT[:, c, :], in0=xpad[:, c, tap:tap + T],
                                               scalar=pcol[:, ROW_CW + tap * NCB + c:ROW_CW + tap * NCB + c + 1],
                                               in1=xcT[:, c, :], op0=ALU.mult, op1=ALU.add)
                    if tap < 2:
                        step(i)
                    else:
                        i.then_inc(conv_done, 1)

            for c in range(NCB):
                convolve(c)
            dve.wait_ge(dt_proj, 1)
            dve.wait_ge(dtw_in, 64)

            def per_head(i):
                return head_rows[:, i, :].unsqueeze(1).broadcast_to([P, TB, H_SSD])

            V.tensor_tensor(dt4[:, 0], ps[:, 4, 0:32].rearrange("p (b h) -> p b h", b=TB), per_head(0),
                            ALU.add).then_inc(dt_raw, 1)
            dve.wait_ge(dt_raw, 1)
            V.scalar_tensor_tensor(out=dt4[:, 1], in0=dt4[:, 0], scalar=-1.0, in1=dt4[:, 0],
                                   op0=ALU.mult, op1=ALU.max).then_inc(dt_raw, 1)
            dve.wait_ge(dt_log, 1)
            step(V.scalar_tensor_tensor(out=dt4[:, 4], in0=dt4[:, 0], scalar=0.0, in1=dt4[:, 3],
                                        op0=ALU.max, op1=ALU.add))
            dve.wait_ge(a_ready, 1)
            V.scalar_tensor_tensor(out=dt4[:, 5], in0=dt4[:, 4], scalar=-1.0, in1=per_head(1),
                                   op0=ALU.mult, op1=ALU.mult).then_inc(da_ready, 1)
            dve.wait_ge(da_ready, 1)

            def d_factor(j):
                if j >= 2:
                    dve.wait_ge(seg_done, j - 1)
                b, q = j // 4, j % 4
                V.tensor_tensor(dfac[:, j % 2, :].rearrange("p (h l) -> p h l", h=4),
                                u_incl[:].unsqueeze(1).broadcast_to([P, 4, P]),
                                dt4[:, 5, b, 4 * q:4 * q + 4].unsqueeze(2).broadcast_to([P, 4, P]),
                                ALU.mult).then_inc(d_ready, 1)

            def g_factor(j):
                dve.wait_ge(e_ready, j + 1)
                if j >= 2:
                    dve.wait_ge(ydiag, j - 1)
                b, q = j // 4, j % 4
                V.tensor_tensor(gfac[:, j % 2, :].rearrange("p (h l) -> p h l", h=4),
                                efac[:, j % 2, :].rearrange("p (h l) -> p h l", h=4),
                                cbm[:, b * GRP + q // 2, :].unsqueeze(1).broadcast_to([P, 4, P]),
                                ALU.mult).then_inc(g_ready, 1)

            dve.wait_ge(consts, 9)
            d_factor(0)
            d_factor(1)
            dve.wait_ge(cb_done, 1)
            V.tensor_tensor(cbm[:], ps[:, 5, :].rearrange("p (c l) -> p c l", c=4),
                            u_incl[:].unsqueeze(1).broadcast_to([P, 4, P]), ALU.mult).then_inc(cbm_ready, 1)
            dve.wait_ge(cbm_ready, 1)
            dve.wait_ge(xs_out, 4)

            def heads(t, width=PD):
                return t.unsqueeze(2).broadcast_to([P, H_SSD, width])

            for b in range(TB):
                i = V.tensor_tensor(xdt[:, b, :].rearrange("p (h d) -> p h d", d=PD),
                                    xs[:, b, :].rearrange("p (h d) -> p h d", d=PD), heads(dt4[:, 4, b, :]), ALU.mult)
                if b == 0:
                    step(i)
                else:
                    i.then_inc(xdt_ready, 1)
            for b in range(TB):
                xb = xs[:, b, :].rearrange("p (h d) -> p h d", d=PD)
                step(V.tensor_tensor(xb, xb, heads(head_rows[:, 2, :]), ALU.mult))

            def take_y(b, half):
                dve.wait_ge(ydiag, 4 * b + 2 * half + 2)
                yy = xs[:, b, half * 512:(half + 1) * 512]
                V.tensor_tensor(yy, ps[:, 4 + half, :], yy, ALU.add).then_inc(y_taken, 1)

            g_factor(0)
            g_factor(1)
            d_factor(2)
            d_factor(3)
            dve.wait_ge(cs_exp, 1)
            V.tensor_tensor(xw.rearrange("p (h d) -> p h d", d=PD), xdt[:, 0, :].rearrange("p (h d) -> p h d", d=PD),
                            heads(dt4[:, 7, 0, :]), ALU.mult).then_inc(xw_ready, 1)
            take_y(0, 0)
            g_factor(2)
            g_factor(3)
            d_factor(4)
            d_factor(5)
            take_y(0, 1)
            g_factor(4)
            g_factor(5)
            d_factor(6)
            d_factor(7)
            take_y(1, 0)
            g_factor(6)
            g_factor(7)
            take_y(1, 1)
            dve.wait_ge(yoff_done, 1)
            dve.wait_ge(ydiag, 8)
            yo = gfac[:].rearrange("p a b -> p (a b)").rearrange("p (h d) -> p h d", d=PD)
            V.tensor_tensor(yo, ps[:, 6:8, :].rearrange("p a (h d) -> p (a h) d", d=PD), heads(dt4[:, 6, 1, :]),
                            ALU.mult).then_inc(yoff_taken, 1)
            dve.wait_ge(yoff_taken, 1)
            dve.wait_ge(y_taken, 4)
            step(V.tensor_tensor(xs[:, 1, :], xs[:, 1, :], gfac[:].rearrange("p a b -> p (a b)"), ALU.add))

            def diag(t):
                return [t[:, e, :].rearrange("p (c t) -> p c t", t=P)[:, 0:3:2, :] for e in range(2)]

            keep = u_strict[:].unsqueeze(1).broadcast_to([P, 2, P])

            def sb_softplus(i):
                dve.wait_ge(sb_log, i + 1)
                step(V.scalar_tensor_tensor(out=sp[i % 2], in0=ps[:, 4 + 2 * (i % 2):6 + 2 * (i % 2), 0:SBC],
                                            scalar=0.0, in1=sp[i % 2], op0=ALU.max, op1=ALU.add))
                a, b = diag(sp[i % 2])
                step(V.tensor_tensor(a, a, keep, ALU.mult))
                V.tensor_tensor(b, b, keep, ALU.mult).then_inc(sb_sp, 1)

            def sb_clip(i):
                dve.wait_ge(sb_acc, i + 1)
                if i >= 2:
                    dve.wait_ge(sb_o, i - 1)
                V.tensor_scalar(wsb[i % 2], ps[:, 4 + 2 * (i % 2):6 + 2 * (i % 2), 0:SBC], 0.0, None,
                                ALU.min).then_inc(sb_min, 1)

            def sb_mask(i):
                dve.wait_ge(sb_w, i + 1)
                a, b = diag(wsb[i % 2])
                step(V.tensor_tensor(a, a, keep, ALU.mult))
                V.tensor_tensor(b, b, keep, ALU.mult).then_inc(sb_wm, 1)

            def sb_take(i):
                dve.wait_ge(sb_o, i + 1)
                V.tensor_copy(sbT[:, i, :], ps[:, 4 + 2 * (i % 2), 0:T]).then_inc(sb_out, 1)

            dve.wait_ge(cb_done, 1)
            dve.wait_ge(yoff_done, 1)
            sb_softplus(0)
            sb_softplus(1)
            dve.wait_ge(silu_z, 1)
            V.tensor_tensor(xs[:], xs[:], z, ALU.mult).then_inc(y_full, 1)
            sb_clip(0)
            sb_clip(1)
            sb_mask(0)
            sb_mask(1)
            sb_take(0)
            sb_take(1)
            dve.wait_ge(rstd, 2)
            for b in range(TB):
                step(V.tensor_scalar(xs[:, b, 0:512], xs[:, b, 0:512], ss[:, 4 + 2 * b:5 + 2 * b], None, ALU.mult))
                V.tensor_scalar(xs[:, b, 512:], xs[:, b, 512:], ss[:, 5 + 2 * b:6 + 2 * b], None,
                                ALU.mult).then_inc(normed, 1)
            sb_softplus(2)
            sb_softplus(3)
            sb_clip(2)
            sb_clip(3)
            sb_mask(2)
            sb_mask(3)
            sb_take(2)
            sb_take(3)
            dve.wait_ge(rstd, 3)
            normalise(memx, memx, 2, blocks=(0, 1))
            take_transposed(TR_Y, nT, ROW_SSD)
            dve.wait_ge(gate_sig, 2)
            for n in range(2):
                c = slice(n * SW, (n + 1) * SW)
                s = FIRST["ssd_out"] + 2 * n
                dve.wait_ge(chunk_used, products_done(s))
                V.tensor_tensor(merged[:, :, c], ps[:, 2 * (s % 2):2 * (s % 2) + 2, :], gates[:, :, c],
                                ALU.mult).then_inc(stripe_out["dve"], 1)
                s += 1
                dve.wait_ge(chunk_used, products_done(s))
                V.tensor_tensor(scr2[:], ps[:, 2 * (s % 2):2 * (s % 2) + 2, :],
                                gates[:, :, D + n * SW:D + (n + 1) * SW], ALU.mult).then_inc(stripe_out["dve"], 1)
                dve.wait_ge(stripe_out["dve"], 2 * n + 2)
                i = V.tensor_tensor(merged[:, :, c], merged[:, :, c], scr2[:], ALU.add)
                i.then_inc(normed, 1)
                dve.wait_ge(normed, NORMED[TR_MEM] + n + 1)
            take_transposed(TR_MEM, memT, ROW_MEM)
            take_transposed(TR_MERGED, nT, None)

            def add_stripes(name):
                for n in range(2):
                    s = FIRST[name] + n
                    hc = h[:, :, n * SW:(n + 1) * SW]
                    dve.wait_ge(chunk_used, products_done(s))
                    V.tensor_tensor(hc, ps[:, 2 * (s % 2):2 * (s % 2) + 2, :], hc,
                                    ALU.add).then_inc(stripe_out["dve"], 1)
                dve.wait_ge(stripe_out["dve"], emptied(FIRST[name] + 1)[1])

            add_stripes("out")
            squares(hn1, h, 8)
            dve.wait_ge(rstd, 4)
            normalise(hn1, h, 8)
            take_transposed(TR_H1, nT, ROW_XATTN)
            for hd in range(H_XA):
                dve.wait_ge(xa_lg, hd + 1)
                V.tensor_reduce(xas[:, 0, 2 * hd:2 * hd + 2], ps[:, 4 + hd, :].rearrange("p (b m) -> p b m", b=TB),
                                AX.X, ALU.max, negate=True).then_inc(xa_max, 1)
            for hd in range(H_XA):
                dve.wait_ge(xa_exp, 2 * hd + 2)
                u = slice(2 * hd, 2 * hd + 2)
                step(V.reciprocal(xas[:, 2, u], xas[:, 1, u]))
                V.tensor_tensor(prob[:, u, :], prob[:, u, :], xas[:, 2, u].unsqueeze(2).broadcast_to([P, TB, T]),
                                ALU.mult).then_inc(xa_prob, 1)
            add_stripes("xo")
            squares(hn2, h, 10)
            dve.wait_ge(rstd, 5)
            normalise(hn2, h, 10)
            take_transposed(TR_H2, nT, ROW_MOE)
            dve.wait_ge(rt_done, 1)
            step(V.tensor_tensor(lg[:], ps[:, 4, 0:TB * NE].rearrange("p (b e) -> p b e", b=TB),
                                 brt[:].unsqueeze(1).broadcast_to([P, TB, NE]), ALU.add))
            for b in range(TB):
                step(V.max(out=top8[:, b, :], in_=lg[:, b, :]))
                step(V.max_index(out=idx8[:, b, :], in_max=top8[:, b, :], in_values=lg[:, b, :]))
            V.tensor_scalar(rsm[:, 0:TB], top8[:, :, 0], -1.0, None, ALU.mult).then_inc(rt_max, 1)
            step(V.tensor_copy(idxf[:], idx8[:, :, 0:TOPK]))
            dve.wait_ge(consts, N_CONST)
            step(V.tensor_tensor(oh4, iota_e[:].unsqueeze(1).unsqueeze(1).broadcast_to([P, TB, TOPK, NE]),
                                 idxf[:].unsqueeze(3).broadcast_to([P, TB, TOPK, NE]), ALU.is_equal))
            V.tensor_reduce(mask[:], oh4.rearrange("p b j e -> p b e j"), AX.X, ALU.add).then_inc(rt_mask, 1)
            dve.wait_ge(rt_exp, 2)
            step(V.reciprocal(rsm[:, 4:4 + TB], rsm[:, 2:2 + TB]))
            step(V.tensor_tensor(g4[:], g4[:], rsm[:, 4:4 + TB].unsqueeze(2).broadcast_to([P, TB, TOPK]), ALU.mult))
            step(V.tensor_tensor(ohg, oh4, g4[:].unsqueeze(3).broadcast_to([P, TB, TOPK, NE]), ALU.mult))
            V.tensor_reduce(gate_d[:], ohg.rearrange("p b j e -> p b e j"), AX.X, ALU.add).then_inc(rt_mask, 1)
            dve.wait_ge(rt_mask, 2)
            dve.wait_ge(rk_done, 1)
            r0 = rankx[:, :, 0:NE]
            step(V.scalar_tensor_tensor(out=r0, in0=ps[:, 5, 0:TB * NE].rearrange("p (b e) -> p b e", b=TB),
                                        scalar=1.0, in1=mask[:], op0=ALU.add, op1=ALU.mult))
            step(V.tensor_scalar(r0, r0, -1.0, None, ALU.add))
            iota_b = iota_s[:].unsqueeze(1).broadcast_to([P, GE, SLOTS])

            def next_onehot(col, ins_sem):
                for b in range(TB):
                    i = V.tensor_tensor(onehot[:, b], iota_b,
                                        rankx[:, b, bass.ds(col, GE)].unsqueeze(2).broadcast_to([P, GE, SLOTS]),
                                        ALU.is_equal)
                    if b == TB - 1:
                        i.then_inc(ins_sem, 1)

            def take_gathered(buf, k0, bank=7):
                g = pcol[:, ROW_MOE + k0:ROW_MOE + k0 + 2].unsqueeze(2).broadcast_to([P, 2, T])
                V.tensor_tensor(buf[:, k0:k0 + 2, :], ps[:, bank, :].rearrange("p (k s) -> p k s", k=2), g,
                                ALU.mult).then_inc(gather_out, 1)

            next_onehot(0, hot_ready)
            V.tensor_reduce(cnt_f[:], ps[:, 5, 2 * NE:3 * NE], AX.X, ALU.max).then_inc(rk_ready, 1)
            dve.wait_ge(rk_ready, 1)
            V.tensor_copy(cnt_i[:], cnt_f[:]).then_inc(rk_ready, 1)
            step(V.memset(rankx[:, :, NPASS * NE:], -1.0))
            step(V.memset(gatex[:, :, NPASS * NE:], 0.0))
            for p_ in range(NPASS):
                c = slice(p_ * NE, (p_ + 1) * NE)
                if p_:
                    step(V.tensor_scalar(rankx[:, :, c], r0, -float(SLOTS * p_), None, ALU.add))
                step(V.tensor_copy(gatex[:, :, c], gate_d[:]))
            step(V.memset(hotT, 0.0))
            V.memset(yb, 0.0).then_inc(yb_ready, 1)
            for k0 in range(0, KD, 2):
                dve.wait_ge(gathered, k0 // 2 + 1)
                take_gathered(xgT[0], k0, 7 - k0 // 2 % 2)

            def experts(it):
                for j in range(BODY):
                    n = it * BODY + j
                    if j % GE == 0:
                        gr = it * 2 + j // GE
                        dve.wait_ge(hot_ready, it * 2 + (j // GE + 1))
                        for b in range(TB):
                            i = V.tensor_tensor(gatehot[:, b],
                                            onehot[:, b].unsqueeze(2).broadcast_to([P, GE, 2, SLOTS]),
                                            gatex[:, b, bass.ds(gr * GE, GE)].unsqueeze(2).unsqueeze(2)
                                            .broadcast_to([P, GE, 2, SLOTS]), ALU.mult)
                        i.then_inc(gatehot_made, 1)
                        dve.wait_ge(chunk_used, it * STEP_CH + (FRONT_CH + (j - 1) * EXP_CH + KD))
                        V.tensor_copy(sel, identx[:, bass.ds(gr * GE, GE)].unsqueeze(2).broadcast_to([NE, GE, SLOTS]))
                        dve.wait_ge(gathered, it * 8 + (j + 4))
                        dve.wait_ge(gatehot_made, it * 2 + (j // GE + 1))
                        next_onehot(gr * GE + GE, hot_ready)
                    dve.wait_ge(chunk_used, it * STEP_CH + (FRONT_CH + j * EXP_CH + KD))
                    V.tensor_scalar(gl, ps[:, 4, :], LIM, None, ALU.min).then_inc(gl_ready, 1)
                    V.tensor_scalar(ul, ps[:, 5, :], LIM, -LIM, ALU.min, ALU.max).then_inc(gu_read, 1)
                    dve.wait_ge(gl_ready, n + 1)
                    dve.wait_ge(gu_read, n + 1)
                    V.scalar_tensor_tensor(out=ul, in0=ul, scalar=1.0, in1=gl, op0=ALU.add,
                                           op1=ALU.mult).then_inc(up_ready, 1)
                    dve.wait_ge(up_ready, n + 1)
                    dve.wait_ge(sg_ready, n + 1)
                    V.tensor_tensor(actv, ul, sg, ALU.mult).then_inc(act_ready, 1)
                    dve.wait_ge(gathered, it * 8 + (j + 5))
                    take_gathered(xgT[1 - j // GE], 2 * (j % GE))
                    dve.wait_ge(chunk_used, it * STEP_CH + (FRONT_CH + (j + 1) * EXP_CH))
                    dve.wait_ge(comb_done, n + 1)
                    V.tensor_copy(yb, ps[:, 6, :]).then_inc(yb_ready, 1)

            with dve.Fori(0, NIT) as g:
                experts(g)
            dve.wait_ge(yb_ready, NE + 1)
            with dve.If(overflow_cond(dve)):
                with dve.Fori(1, NPASS) as p_:
                    with dve.Fori(0, NIT) as g:
                        experts(p_ * NIT + g)
                dve.wait_ge(yb_ready, NPASS * NE + 1)
            V.tensor_copy(cnt_f[:], cnt_i[:]).then_inc(yb_last, 1)
            for b in range(TB):
                dve.wait_ge(y_done, b + 1)
                V.tensor_tensor(h[:, b, :], ps[:, 2 * b:2 * b + 2, :].rearrange("p a d -> p (a d)"), h[:, b, :],
                                ALU.add).then_inc(h_full, 1)
            dve.wait_ge(h_full, 2)
            squares(xn, h, 12)
            dve.wait_ge(rstd, 6)
            dve.wait_ge(gf_in, 16)
            for b in range(TB):
                V.scalar_tensor_tensor(out=xn[:, b, :], in0=h[:, b, :], scalar=ss[:, 12 + b:13 + b], in1=gfin,
                                       op0=ALU.mult, op1=ALU.mult).then_inc(out_ready, 1)


_INS = ["x", "mem", "g_mix", "w_in", "conv_w", "conv_b", "dt_bias", "a_log", "d_skip", "g_ssd", "w_ssd_out",
        "w_sb_out", "w_out", "g_xattn", "g_mem", "w_xq", "w_xkv", "w_xo", "g_moe", "w_router", "b_router",
        "w_gu", "b_gu", "w_down", "b_down", "g_final"]


def kernel(**inputs):
    import concourse.bacc as bacc
    from concourse.bass_utils import run_bass_kernel_spmd

    nc = bacc.Bacc("TRN2", target_bir_lowering=False, num_devices=1)
    arrays, args = {}, []
    for name in _INS:
        a = np.ascontiguousarray(inputs[name])
        arrays[f"in_{name}"] = a
        args.append(nc.dram_tensor(f"in_{name}", a.shape, mybir.dt.from_np(a.dtype), kind="ExternalInput").ap())
    args.append(nc.dram_tensor("out_h", (1, T, D), F32, kind="ExternalOutput").ap())
    build(nc, *args)
    r = run_bass_kernel_spmd(nc, [arrays], core_ids=[0])
    return r.results[0]["out_h"]
```
